# Optimizing a Trainium2 kernel written in Bass

```python
import math
import jax, jax.numpy as jnp
from jax import lax
import numpy as np

D_MODEL = 1024
BATCH = 1
SEQ = 256
DEPTH = 1

D_RNN = 1024
RNN_BLOCKS = 16
RNN_BW = D_RNN // RNN_BLOCKS
CONV_W = 4
LRU_C = 8.0
N_HEADS = 16
N_KV = 4
HEAD_DIM = 64
GROUP = N_HEADS // N_KV
WINDOW = 128
BLOCK_Q = 128
Q_DIM = N_HEADS * HEAD_DIM
KV_DIM = N_KV * HEAD_DIM
N_EXPERTS = 32
TOP_K = 4
D_FF = 1024
SWIGLU_LIMIT = 7.0
SWIGLU_ALPHA = 1.702
MOE_BLOCK = 128
EPS = 1e-6
SPLITS = (D_RNN, D_RNN, Q_DIM, KV_DIM, KV_DIM, D_MODEL, D_MODEL)
D_IN = sum(SPLITS)


def rmsnorm(x, g):
    xf = x.astype(jnp.float32)
    y = xf * lax.rsqrt(jnp.mean(xf * xf, axis=-1, keepdims=True) + EPS)
    return (y * g.astype(jnp.float32)).astype(x.dtype)

def causal_depthwise_conv(x, w, b):
    S = x.shape[1]
    xp = jnp.pad(x, ((0, 0), (CONV_W - 1, 0), (0, 0)))
    y = b
    for kk in range(CONV_W):
        y = y + xp[:, kk:kk + S] * w[kk]
    return y

def rg_lru(x, w_a, b_a, w_x, b_x, lam):
    B, S, _ = x.shape
    xb = x.reshape(B, S, RNN_BLOCKS, RNN_BW)
    gate_r = jax.nn.sigmoid(jnp.einsum('bshi,hij->bshj', xb, w_a).reshape(B, S, D_RNN) + b_a)
    gate_i = jax.nn.sigmoid(jnp.einsum('bshi,hij->bshj', xb, w_x).reshape(B, S, D_RNN) + b_x)
    log_a = -LRU_C * gate_r.astype(jnp.float32) * jax.nn.softplus(-lam.astype(jnp.float32))
    a = jnp.exp(log_a)
    mult = jnp.sqrt(-jnp.expm1(2.0 * log_a))
    reset = (jnp.arange(S) == 0)[None, :, None]
    mult = jnp.where(reset, 1.0, mult)
    bterm = (x * gate_i).astype(jnp.float32) * mult

    def combine(left, right):
        a1, b1 = left
        a2, b2 = right
        return a1 * a2, a2 * b1 + b2

    _, h = lax.associative_scan(combine, (a, bterm), axis=1)
    return h.astype(x.dtype)

def alibi_slopes():
    return np.array([2.0 ** (-8.0 * (h + 1) / N_HEADS) for h in range(N_HEADS)], dtype=np.float32)

def swa_sink_attention(q, k, v, sinks):
    B, S = q.shape[0], q.shape[1]
    nb = S // BLOCK_Q
    qb = q.reshape(B, nb, BLOCK_Q, N_KV, GROUP, HEAD_DIM)
    pad = ((0, 0), (BLOCK_Q, 0), (0, 0), (0, 0))
    kb = jnp.pad(k, pad).reshape(B, nb + 1, BLOCK_Q, N_KV, HEAD_DIM)
    vb = jnp.pad(v, pad).reshape(B, nb + 1, BLOCK_Q, N_KV, HEAD_DIM)
    k_band = jnp.concatenate([kb[:, :-1], kb[:, 1:]], axis=2)
    v_band = jnp.concatenate([vb[:, :-1], vb[:, 1:]], axis=2)
    s = jnp.einsum('bnqkgd,bnckd->bnkgqc', qb, k_band,
                   preferred_element_type=jnp.float32) * (HEAD_DIM ** -0.5)
    qi = jnp.arange(BLOCK_Q)[:, None]
    ci = jnp.arange(2 * BLOCK_Q)[None, :]
    dist = qi + BLOCK_Q - ci
    kpos = jnp.arange(nb)[:, None, None] * BLOCK_Q - BLOCK_Q + ci[None]
    valid = (dist >= 0) & (dist < WINDOW) & (kpos >= 0)
    slopes = jnp.asarray(alibi_slopes()).reshape(N_KV, GROUP)[:, :, None, None]
    s = s - slopes * dist.astype(jnp.float32)
    s = jnp.where(valid[None, :, None, None], s, -jnp.inf)
    sink = sinks.astype(jnp.float32).reshape(N_KV, GROUP)[:, :, None, None]
    m = jnp.maximum(jnp.max(s, axis=-1, keepdims=True), sink)
    p = jnp.exp(s - m)
    denom = jnp.sum(p, axis=-1, keepdims=True) + jnp.exp(sink - m)
    o = jnp.einsum('bnkgqc,bnckd->bnqkgd', (p / denom).astype(v.dtype), v_band)
    return o.reshape(B, S, Q_DIM)

def clamped_swiglu(hid):
    x_glu = jnp.minimum(hid[..., ::2], SWIGLU_LIMIT)
    x_lin = jnp.clip(hid[..., 1::2], -SWIGLU_LIMIT, SWIGLU_LIMIT)
    return x_glu * jax.nn.sigmoid(SWIGLU_ALPHA * x_glu) * (x_lin + 1.0)

def moe_ffn(h, router_w, router_b, w1, b1, w2, b2):
    B, S, D = h.shape
    N = B * S
    xt = h.reshape(N, D)
    logits = (xt @ router_w + router_b).astype(jnp.float32)
    top_v, top_e = lax.top_k(logits, TOP_K)
    gates = jax.nn.softmax(top_v, axis=-1)
    A = N * TOP_K
    e_flat = top_e.reshape(A)
    g_flat = gates.reshape(A)
    tok = jnp.arange(A, dtype=jnp.int32) // TOP_K
    order = jnp.argsort(e_flat, stable=True)
    e_s, tok_s, g_s = e_flat[order], tok[order], g_flat[order]
    counts = jnp.bincount(e_flat, length=N_EXPERTS)
    starts = jnp.cumsum(counts) - counts
    padded = ((counts + MOE_BLOCK - 1) // MOE_BLOCK) * MOE_BLOCK
    pend = jnp.cumsum(padded)
    pstart = pend - padded
    dest = pstart[e_s] + jnp.arange(A, dtype=jnp.int32) - starts[e_s]
    P = A + N_EXPERTS * MOE_BLOCK
    nblk = P // MOE_BLOCK
    tok_buf = jnp.full((P,), N, dtype=jnp.int32).at[dest].set(tok_s)
    g_buf = jnp.zeros((P,), jnp.float32).at[dest].set(g_s)
    blk_e = jnp.clip(jnp.searchsorted(pend, jnp.arange(nblk, dtype=jnp.int32) * MOE_BLOCK,
                                      side='right'), 0, N_EXPERTS - 1)
    x_pad = jnp.concatenate([xt, jnp.zeros((1, D), xt.dtype)], axis=0)
    xb = x_pad[tok_buf].reshape(nblk, MOE_BLOCK, D)

    def expert_block(args):
        xblk, e = args
        act = clamped_swiglu(xblk @ w1[e] + b1[e])
        return act @ w2[e] + b2[e]

    yb = lax.map(expert_block, (xb, blk_e)).reshape(P, D)
    yb = yb * g_buf[:, None].astype(yb.dtype)
    out = jax.ops.segment_sum(yb, tok_buf, num_segments=N + 1)[:N]
    return out.reshape(B, S, D)

def first_inputs(seed: int = 0) -> dict:
    key = jax.random.key(seed)
    ks = jax.random.split(key, 24)
    f32 = jnp.float32
    L = DEPTH

    def nrm(k, shape, scale):
        return jax.random.normal(k, shape, f32) * scale

    def gain(k, shape):
        return 1.0 + 0.05 * jax.random.normal(k, shape, f32)

    u = jax.random.uniform(ks[12], (L, D_RNN), f32, 0.9, 0.999)
    sig = u ** (1.0 / LRU_C)
    rg_lambda = jnp.log(sig) - jnp.log1p(-sig)
    return {
        "x": nrm(ks[0], (BATCH, SEQ, D_MODEL), 1.0),
        "c": nrm(ks[1], (BATCH, D_MODEL), 1.0),
        "w_ada": nrm(ks[2], (L, D_MODEL, 6 * D_MODEL), 0.5 * D_MODEL ** -0.5),
        "b_ada": nrm(ks[3], (L, 6 * D_MODEL), 0.02),
        "norm_pre_mix": gain(ks[4], (L, D_MODEL)),
        "norm_post_mix": gain(ks[5], (L, D_MODEL)),
        "norm_pre_ffn": gain(ks[6], (L, D_MODEL)),
        "norm_post_ffn": gain(ks[7], (L, D_MODEL)),
        "w_in": nrm(ks[8], (L, D_MODEL, D_IN), D_MODEL ** -0.5),
        "b_in": nrm(ks[9], (L, D_IN), 0.02),
        "conv_w": nrm(ks[10], (L, CONV_W, D_RNN), CONV_W ** -0.5),
        "conv_b": nrm(ks[11], (L, D_RNN), 0.02),
        "rg_w_a": nrm(ks[13], (L, RNN_BLOCKS, RNN_BW, RNN_BW), RNN_BW ** -0.5),
        "rg_b_a": nrm(ks[14], (L, D_RNN), 0.02),
        "rg_w_x": nrm(ks[15], (L, RNN_BLOCKS, RNN_BW, RNN_BW), RNN_BW ** -0.5),
        "rg_b_x": nrm(ks[16], (L, D_RNN), 0.02),
        "rg_lambda": rg_lambda,
        "attn_sinks": nrm(ks[17], (L, N_HEADS), 0.5),
        "w_o_rnn": nrm(ks[18], (L, D_RNN, D_MODEL), D_RNN ** -0.5),
        "w_o_attn": nrm(ks[19], (L, Q_DIM, D_MODEL), Q_DIM ** -0.5),
        "w_out": nrm(ks[20], (L, D_MODEL, D_MODEL), D_MODEL ** -0.5),
        "router_w": nrm(ks[21], (L, D_MODEL, N_EXPERTS), D_MODEL ** -0.5),
        "router_b": nrm(ks[22], (L, N_EXPERTS), 0.01),
        "moe_w1": nrm(jax.random.fold_in(ks[23], 0), (L, N_EXPERTS, D_MODEL, 2 * D_FF), D_MODEL ** -0.5),
        "moe_b1": nrm(jax.random.fold_in(ks[23], 1), (L, N_EXPERTS, 2 * D_FF), 0.02),
        "moe_w2": nrm(jax.random.fold_in(ks[23], 2), (L, N_EXPERTS, D_FF, D_MODEL), D_FF ** -0.5),
        "moe_b2": nrm(jax.random.fold_in(ks[23], 3), (L, N_EXPERTS, D_MODEL), 0.02),
    }

def first_block(x, c, w_ada, b_ada, norm_pre_mix, norm_post_mix, norm_pre_ffn, norm_post_ffn,
              w_in, b_in, conv_w, conv_b, rg_w_a, rg_b_a, rg_w_x, rg_b_x, rg_lambda,
              attn_sinks, w_o_rnn, w_o_attn, w_out, router_w, router_b,
              moe_w1, moe_b1, moe_w2, moe_b2):
    B, S, _ = x.shape
    split_points = np.cumsum(np.array(SPLITS))[:-1].tolist()
    for layer in range(DEPTH):
        ada = (jax.nn.silu(c) @ w_ada[layer] + b_ada[layer])[:, None, :]
        sh1, sc1, g1, sh2, sc2, g2 = jnp.split(ada, 6, axis=-1)

        h = rmsnorm(x, norm_pre_mix[layer]) * (1.0 + sc1) + sh1
        proj = h @ w_in[layer] + b_in[layer]
        xr, gr, q, k, v, gate_r, gate_a = jnp.split(proj, split_points, axis=-1)
        xr = causal_depthwise_conv(xr, conv_w[layer], conv_b[layer])
        y_rnn = rg_lru(xr, rg_w_a[layer], rg_b_a[layer], rg_w_x[layer], rg_b_x[layer],
                       rg_lambda[layer]) * jax.nn.gelu(gr)
        y_att = swa_sink_attention(q.reshape(B, S, N_HEADS, HEAD_DIM),
                                   k.reshape(B, S, N_KV, HEAD_DIM),
                                   v.reshape(B, S, N_KV, HEAD_DIM), attn_sinks[layer])
        merged = (jax.nn.sigmoid(gate_r) * (y_rnn @ w_o_rnn[layer])
                  + jax.nn.sigmoid(gate_a) * (y_att @ w_o_attn[layer]))
        mix = merged @ w_out[layer]
        x = x + g1 * rmsnorm(mix, norm_post_mix[layer])

        h = rmsnorm(x, norm_pre_ffn[layer]) * (1.0 + sc2) + sh2
        ff = moe_ffn(h, router_w[layer], router_b[layer], moe_w1[layer], moe_b1[layer],
                     moe_w2[layer], moe_b2[layer])
        x = x + g2 * rmsnorm(ff, norm_post_ffn[layer])
    return x


DEPTH_2 = 2

N_MIXERS = 2
N_CONV_LAYERS = (DEPTH_2 + 1) // 2
N_ATTN_LAYERS = DEPTH_2 // 2
D_FF_2 = 2816
CONV_WIDTH = 3
N_HEADS_2 = D_MODEL // HEAD_DIM
DILATION_GROUPS = ((128, 1), (512, 4), (2048, 16))
N_GROUPS = len(DILATION_GROUPS)
BLOCK = 128
N_BUCKETS = 32
MAX_EXACT = N_BUCKETS // 2
MAX_DISTANCE = 2048
RMS_EPS = 1e-6
NEG_INF = -1e30


def rmsnorm_2(x, g):
    xf = x.astype(jnp.float32)
    y = xf * lax.rsqrt(jnp.mean(xf * xf, axis=-1, keepdims=True) + RMS_EPS) * g.astype(jnp.float32)
    return y.astype(x.dtype)

def swiglu(h, w_in, w_out):
    gate, up = jnp.split(h @ w_in, 2, axis=-1)
    return (jax.nn.silu(gate) * up) @ w_out

def short_conv_mixer(h, w_in, w_conv, w_out):
    b_gate, c_gate, u = jnp.split(h @ w_in, 3, axis=-1)
    v = c_gate * u
    T = v.shape[1]
    vp = jnp.pad(v, ((0, 0), (CONV_WIDTH - 1, 0), (0, 0)))
    conv = sum(w_conv[lag] * vp[:, CONV_WIDTH - 1 - lag:CONV_WIDTH - 1 - lag + T]
               for lag in range(CONV_WIDTH))
    return (b_gate * conv) @ w_out

def t5_bucket(dist):
    is_small = dist < MAX_EXACT
    nf = jnp.maximum(dist, 1).astype(jnp.float32)
    large = MAX_EXACT + (jnp.log(nf / MAX_EXACT) / math.log(MAX_DISTANCE / MAX_EXACT)
                         * (N_BUCKETS - MAX_EXACT)).astype(jnp.int32)
    large = jnp.minimum(large, N_BUCKETS - 1)
    return jnp.where(is_small, dist, large)

def band_bias(rel_bias_g, dilation, n_steps):
    i = jnp.arange(BLOCK)[:, None]
    j = jnp.arange(2 * BLOCK)[None, :]
    step = BLOCK + i - j
    in_band = (step >= 0) & (step <= n_steps)
    bucket = t5_bucket(jnp.clip(step, 0, n_steps) * dilation)
    bias = rel_bias_g[bucket]
    return jnp.transpose(bias, (2, 0, 1)).astype(jnp.float32), in_band

def dilated_group(q, k, v, bias, in_band, dilation):
    B, T, H, Dh = q.shape
    span = dilation * BLOCK
    Tp = -(-T // span) * span
    L = Tp // dilation
    Lb = L // BLOCK

    def to_sub(a):
        a = jnp.pad(a, ((0, 0), (0, Tp - T), (0, 0), (0, 0))).reshape(B, L, dilation, H, Dh)
        return jnp.transpose(a, (0, 2, 1, 3, 4)).reshape(B, dilation, Lb, BLOCK, H, Dh)

    def with_prev(a):
        prev = jnp.pad(a, ((0, 0), (0, 0), (1, 0), (0, 0), (0, 0), (0, 0)))[:, :, :-1]
        return jnp.concatenate([prev, a], axis=3)

    qs = to_sub(q)
    kb = with_prev(to_sub(k))
    vb = with_prev(to_sub(v))
    logits = jnp.einsum('bsnqhd,bsnkhd->bsnhqk', qs, kb) + bias
    n_idx = jnp.arange(Lb)[:, None, None, None]
    j_idx = jnp.arange(2 * BLOCK)[None, None, None, :]
    valid = in_band[None, None] & ~((n_idx == 0) & (j_idx < BLOCK))
    logits = jnp.where(valid, logits, NEG_INF)
    m = jnp.max(logits, axis=-1, keepdims=True)
    p = jnp.exp(logits - m)
    s = jnp.sum(p, axis=-1, keepdims=True)
    o = jnp.einsum('bsnhqk,bsnkhd->bsnqhd', p, vb)
    o = o / jnp.transpose(s, (0, 1, 2, 4, 3, 5))
    lse = jnp.transpose((m + jnp.log(s))[..., 0], (0, 1, 2, 4, 3))

    def from_sub(a):
        rest = a.shape[4:]
        a = a.reshape((B, dilation, L) + rest)
        a = jnp.moveaxis(a, 1, 2).reshape((B, Tp) + rest)
        return a[:, :T]

    return from_sub(o), from_sub(lse)

def dilated_attention_mixer(h, w_qkv, q_gain, k_gain, w_out, rel_bias):
    B, T, _ = h.shape
    qkv = (h @ w_qkv).reshape(B, T, N_GROUPS, 3, N_HEADS_2, HEAD_DIM)
    outs, lses = [], []
    for g, (window, dilation) in enumerate(DILATION_GROUPS):
        q = rmsnorm_2(qkv[:, :, g, 0].astype(jnp.float32), q_gain[g]) * (HEAD_DIM ** -0.5)
        k = rmsnorm_2(qkv[:, :, g, 1].astype(jnp.float32), k_gain[g])
        v = qkv[:, :, g, 2].astype(jnp.float32)
        bias, in_band = band_bias(rel_bias[:, g * N_HEADS_2:(g + 1) * N_HEADS_2], dilation, window // dilation)
        o, lse = dilated_group(q, k, v, bias, in_band, dilation)
        outs.append(o)
        lses.append(lse)
    wts = jax.nn.softmax(jnp.stack(lses), axis=0)
    o = jnp.einsum('gbth,gbthd->bthd', wts, jnp.stack(outs))
    return o.reshape(B, T, N_HEADS_2 * HEAD_DIM).astype(h.dtype) @ w_out

def second_inputs(seed: int = 0) -> dict:
    key = jax.random.key(seed)
    ks = jax.random.split(key, 16)
    f32 = jnp.float32

    def w(k, shape, fan_in):
        return jax.random.normal(k, shape, f32) * (fan_in ** -0.5)

    def gain(k, shape):
        return 1.0 + 0.05 * jax.random.normal(k, shape, f32)

    return {
        "x": jax.random.normal(ks[0], (BATCH, SEQ, D_MODEL), f32),
        "norm_ffn1": gain(ks[1], (DEPTH_2, D_MODEL)),
        "ffn1_w_in": w(ks[2], (DEPTH_2, D_MODEL, 2 * D_FF_2), D_MODEL),
        "ffn1_w_out": w(ks[3], (DEPTH_2, D_FF_2, D_MODEL), D_FF_2),
        "norm_mix": gain(ks[4], (DEPTH_2, D_MODEL)),
        "conv_w_in": w(ks[5], (N_CONV_LAYERS, D_MODEL, 3 * D_MODEL), D_MODEL),
        "conv_w": w(ks[6], (N_CONV_LAYERS, CONV_WIDTH, D_MODEL), CONV_WIDTH),
        "conv_w_out": w(ks[7], (N_CONV_LAYERS, D_MODEL, D_MODEL), D_MODEL),
        "attn_w_qkv": w(ks[8], (N_ATTN_LAYERS, D_MODEL, N_GROUPS * 3 * N_HEADS_2 * HEAD_DIM), D_MODEL),
        "attn_q_gain": gain(ks[9], (N_ATTN_LAYERS, N_GROUPS, HEAD_DIM)),
        "attn_k_gain": gain(ks[10], (N_ATTN_LAYERS, N_GROUPS, HEAD_DIM)),
        "attn_w_out": w(ks[11], (N_ATTN_LAYERS, N_HEADS_2 * HEAD_DIM, D_MODEL), N_HEADS_2 * HEAD_DIM),
        "rel_bias": 0.5 * jax.random.normal(ks[12], (N_BUCKETS, N_GROUPS * N_HEADS_2), f32),
        "norm_ffn2": gain(ks[13], (DEPTH_2, D_MODEL)),
        "ffn2_w_in": w(ks[14], (DEPTH_2, D_MODEL, 2 * D_FF_2), D_MODEL),
        "ffn2_w_out": w(ks[15], (DEPTH_2, D_FF_2, D_MODEL), D_FF_2),
    }

def second_block(x, norm_ffn1, ffn1_w_in, ffn1_w_out, norm_mix, conv_w_in, conv_w, conv_w_out,
              attn_w_qkv, attn_q_gain, attn_k_gain, attn_w_out, rel_bias,
              norm_ffn2, ffn2_w_in, ffn2_w_out):
    h = x
    for i in range(DEPTH_2):
        h = h + 0.5 * swiglu(rmsnorm_2(h, norm_ffn1[i]), ffn1_w_in[i], ffn1_w_out[i])
        hn = rmsnorm_2(h, norm_mix[i])
        j = i // N_MIXERS
        if i % N_MIXERS == 0:
            mix = short_conv_mixer(hn, conv_w_in[j], conv_w[j], conv_w_out[j])
        else:
            mix = dilated_attention_mixer(hn, attn_w_qkv[j], attn_q_gain[j], attn_k_gain[j],
                                          attn_w_out[j], rel_bias)
        h = h + mix
        h = h + 0.5 * swiglu(rmsnorm_2(h, norm_ffn2[i]), ffn2_w_in[i], ffn2_w_out[i])
    return h


def setup_inputs(seed=0):
    out = dict(first_inputs(seed))
    for name, value in second_inputs(seed + 1).items():
        if name != "x":
            out[name + "_2"] = value
    return out


def reference(
    x, c, w_ada, b_ada, norm_pre_mix, norm_post_mix, norm_pre_ffn, norm_post_ffn, w_in, b_in,
    conv_w, conv_b, rg_w_a, rg_b_a, rg_w_x, rg_b_x, rg_lambda, attn_sinks, w_o_rnn, w_o_attn,
    w_out, router_w, router_b, moe_w1, moe_b1, moe_w2, moe_b2, norm_ffn1_2, ffn1_w_in_2,
    ffn1_w_out_2, norm_mix_2, conv_w_in_2, conv_w_2, conv_w_out_2, attn_w_qkv_2, attn_q_gain_2,
    attn_k_gain_2, attn_w_out_2, rel_bias_2, norm_ffn2_2, ffn2_w_in_2, ffn2_w_out_2,
):
    x = first_block(
        x, c, w_ada, b_ada, norm_pre_mix, norm_post_mix, norm_pre_ffn, norm_post_ffn, w_in,
        b_in, conv_w, conv_b, rg_w_a, rg_b_a, rg_w_x, rg_b_x, rg_lambda, attn_sinks, w_o_rnn,
        w_o_attn, w_out, router_w, router_b, moe_w1, moe_b1, moe_w2, moe_b2,
    )
    return second_block(
        x, norm_ffn1_2, ffn1_w_in_2, ffn1_w_out_2, norm_mix_2, conv_w_in_2, conv_w_2,
        conv_w_out_2, attn_w_qkv_2, attn_q_gain_2, attn_k_gain_2, attn_w_out_2, rel_bias_2,
        norm_ffn2_2, ffn2_w_in_2, ffn2_w_out_2,
    )


_drawn_inputs = setup_inputs


def setup_inputs(seed=0):
    import zlib

    import numpy as np

    out = dict(_drawn_inputs(seed))
    spreads = {}
    factors = {'norm_post_ffn': 2.717,
     'rg_b_a': 8.0,
     'rg_b_x': 5.773,
     'moe_b1': 5.608,
     'moe_b2': 6.661,
     'attn_q_gain_2': 8.0,
     'attn_k_gain_2': 8.0,
     'norm_ffn2_2': 2.806,
     'rel_bias_2': 2.982}
    for name, (base, spread) in spreads.items():
        noise = np.random.default_rng([zlib.crc32(name.encode()), seed]).standard_normal(out[name].shape)
        drawn = base * np.exp(spread * noise) if base else spread * noise
        out[name] = __import__('jax').numpy.asarray(drawn.astype(out[name].dtype))
    for name, factor in factors.items():
        out[name] = (out[name] * factor).astype(out[name].dtype)
    return out
```

```python
import math
from contextlib import contextmanager

import numpy as np

import concourse.bass as bass
from concourse import mybir

P = 128
D = 1024
S = 256
DC = D // P
TT = S // P
KV = 4
HEADS = 16
HD = 64
NE = 32
TOPK = 4
FF = 1024
FF2 = 2816
FC = FF2 // P
SLOTS = 64
BUCKETS = 32
N_GROUPS = 3
EPS = 1e-6
NEG = -1e30
CONV_W = 4
CONV_W2 = 3

PARAMS = [("c", 8), ("b_ada", 48), ("norm_pre_mix", 8), ("norm_post_mix", 8), ("norm_pre_ffn", 8),
          ("norm_post_ffn", 8), ("b_in", 44), ("conv_w", 32), ("conv_b", 8), ("rg_b_a", 8),
          ("rg_b_x", 8), ("rg_lambda", 8), ("norm_ffn1_2", 16), ("norm_mix_2", 16),
          ("norm_ffn2_2", 16), ("conv_w_2", 24), ("attn_q_gain_2", 3), ("attn_k_gain_2", 3)]
COL = {}
NPAR = 0
for _name, _n in PARAMS:
    COL[_name] = NPAR
    NPAR += _n


def t5_bucket(dist):
    large = 16 + (np.log(np.maximum(dist, 1).astype(np.float32) / 16) / math.log(2048 / 16) * 16).astype(np.int32)
    return np.where(dist < 16, dist, np.minimum(large, BUCKETS - 1))


def constants():
    f = np.float32
    ident = np.eye(P, dtype=f)
    flip = ident[:, ::-1].copy()
    before = np.triu(np.ones((P, P), f), 1)
    slot = np.tile(np.arange(SLOTS, dtype=f), (P, 2))
    small = np.concatenate([ident, flip, before, slot], axis=1)
    q = np.arange(P)[:, None]
    c = np.arange(2 * P)[None, :]
    dist = q + P - c
    ok = (dist >= 0) & (dist < 128)
    slopes = np.array([2.0 ** (-8.0 * (h + 1) / HEADS) for h in range(HEADS)], f)
    alibi = np.where(ok[:, None, :], -(slopes[None, :, None] * dist[:, None, :].astype(f)), NEG).astype(f)
    d = 255 - np.arange(384)
    onehot = np.zeros((BUCKETS + 1, N_GROUPS, 384), f)
    for g, (window, dil) in enumerate(((128, 1), (512, 4), (2048, 16))):
        seen = (d >= 0) & (d % dil == 0) & (d <= window)
        b = t5_bucket(np.clip(d, 0, window))
        for j in range(384):
            onehot[b[j] if seen[j] else BUCKETS, g, j] = 1.0
    return small, alibi.reshape(P, HEADS * 2 * P), onehot.reshape(BUCKETS + 1, N_GROUPS * 384)


class Steps:

    def __init__(self, eng, sem):
        self.eng, self.sem, self.n = eng, sem, 0
        self.k = 0

    def mark(self, ins):
        ins.then_inc(self.sem, 1)
        self.n = self.n + 1
        self.k += 1

    def wait(self):
        self.eng.wait_ge(self.sem, self.n)

    def link(self, ins):
        self.mark(ins)
        self.wait()

    @contextmanager
    def loop(self, start, end, per):
        base, k = self.n, self.k
        with self.eng.Fori(start, end) as i:
            self.n = base + (i - start) * per
            yield i
        assert self.k - k == per, (self.k - k, per)
        self.n = base + (end - start) * per


class Layer:

    def __init__(self, name, tiles, kc, src, tok=False, unroll=None):
        self.name, self.T, self.kc, self.src, self.tok = name, tiles, kc, src, tok
        self.tpg = 2 if kc == DC else 1
        self.slots = 4 if kc == DC else 2
        self.U = unroll or 4 * self.tpg
        self.G = tiles // self.tpg
        self.gu = self.U // self.tpg


def units(eng, lo, hi, unroll, body):
    t = lo
    while t < hi:
        whole = (hi - t) // unroll
        if t % unroll == 0 and whole >= 2:
            with eng.Fori(t // unroll, t // unroll + whole) as i:
                for u in range(unroll):
                    body(i, u)
            t += whole * unroll
        else:
            body(t // unroll, t % unroll)
            t += 1


def block_program(nc, A, out, phases="ABCD"):
    f32, f32r, i32, u32 = mybir.dt.float32, mybir.dt.float32r, mybir.dt.int32, mybir.dt.uint32
    ALU, ACT, AX = mybir.AluOpType, mybir.ActivationFunctionType, mybir.AxisListType
    ds = bass.ds

    top = nc.sbuf_usable_end
    KB = 1024

    class Region:

        def __init__(self, offset):
            self.o = offset

        def __call__(self, name, free, dt=f32):
            n = (int(np.prod(free)) * 4 + 31) // 32 * 32
            assert self.o + n <= top, (name, self.o + n, top)
            t = nc.alloc_sbuf_tensor_at(name, [P] + list(free), dt, offset=self.o)
            self.o += n
            return t

    r0 = Region((nc.sbuf_base + 63) // 64 * 64)
    PRM = r0("PRM", [NPAR])
    SM = r0("SM", [4 * P])
    IDENT, FLIP, BEFORE, SLOT = (SM[:, i * P:(i + 1) * P] for i in range(4))
    MEAN = r0("MEAN", [P])
    ONE = r0("ONE", [P])
    EPSC = r0("EPSC", [1])
    XT = r0("XT", [DC, S])
    ADA = r0("ADA", [48])
    ADV = r0("ADV", [4, DC])
    RS = r0("RS", [S])
    SD = r0("SD", [S])
    LAMV = r0("LAMV", [6, DC])
    SINK = r0("SINK", [2, HEADS])
    CSIL = r0("CSIL", [DC])
    STAT = r0("STAT", [8, 2])
    QKG = r0("QKG", [6])
    RAW = [r0(f"RAW{s}", [FC * P]) for s in range(4)]
    body0 = r0.o
    WHI = r0("WHI", [48 * P], f32r)
    WLO = r0("WLO", [48 * P], f32r)
    hn0 = r0.o
    HNH = r0("HNH", [DC, S], f32r)
    HNL = r0("HNL", [DC, S], f32r)
    work0 = r0.o

    PS = nc.alloc_psum_tensor("PS", [P, 8 * 512], f32)
    bank = [PS[:, b * 512:(b + 1) * 512] for b in range(8)]
    bias_rows = nc.dram_tensor("bias_rows", [N_GROUPS, HEADS, 384], f32, kind="Internal").ap()

    made = {}

    def sem(name):
        if name not in made:
            made[name] = nc.alloc_semaphore(name)
        return made[name]

    raw_loaded = [sem(f"raw_loaded{s}") for s in range(4)]
    hi_done, lo_done = sem("hi_done"), sem("lo_done")
    mm_done, evacuated = sem("mm_done"), sem("evacuated")

    def cols(w, c0=0, width=256, step=0):
        v = w.rearrange("(k p) n -> p k n", p=P)

        def src(i, gu, per_turn):
            move = step or width * per_turn
            if isinstance(i, int):
                return v[:, :, i * move + c0 + width * gu:i * move + c0 + width * (gu + 1)]
            return v[:, :, ds(i * move + (c0 + width * gu), width)]
        return src

    layers = []
    if "A" in phases:
        layers += [Layer("win", 44, DC, cols(A["w_in"][0])),
                   Layer("wor", 8, DC, cols(A["w_o_rnn"][0])),
                   Layer("woa", 8, DC, cols(A["w_o_attn"][0])),
                   Layer("wout", 8, DC, cols(A["w_out"][0]))]

    def ffn_layers(tag, w_in, w_out):
        return [Layer(f"gate{tag}", FC, DC, cols(w_in)),
                Layer(f"up{tag}", FC, DC, cols(w_in, FF2)),
                Layer(f"down{tag}", DC, FC, cols(w_out, 0, P))]

    if "C" in phases:
        layers += ffn_layers("1_0", A["ffn1_w_in_2"][0], A["ffn1_w_out_2"][0])
        layers += [Layer("conv_cu", 16, DC, cols(A["conv_w_in_2"][0], D)),
                   Layer("conv_b", 8, DC, cols(A["conv_w_in_2"][0], 0)),
                   Layer("conv_out", 8, DC, cols(A["conv_w_out_2"][0]))]
        layers += ffn_layers("2_0", A["ffn2_w_in_2"][0], A["ffn2_w_out_2"][0])
    if "D" in phases:
        layers += ffn_layers("1_1", A["ffn1_w_in_2"][1], A["ffn1_w_out_2"][1])
        qkv = A["attn_w_qkv_2"][0]
        layers += [Layer("qk", 48, DC, cols(qkv, 0, 256, 3 * D), tok=True, unroll=16),
                   Layer("v", 24, DC, cols(qkv, 2 * D, 256, 3 * D), tok=True),
                   Layer("attn_out", 8, DC, cols(A["attn_w_out_2"][0]))]
        layers += ffn_layers("2_1", A["ffn2_w_in_2"][1], A["ffn2_w_out_2"][1])
    fresh = {layers[0].name} if layers else set()
    if "B" in phases and "C" in phases:
        fresh.add("gate1_0")
    group_end = []
    n = g = 0
    for idx, L in enumerate(layers):
        L.n0, L.g0, L.idx = n, g, idx
        group_end += [n + (j + 1) * L.tpg for j in range(L.G)]
        n, g = n + L.T, g + L.G
    by_name = {L.name: L for L in layers}

    def load_layer(sp, L):
        def one(i, gu):
            s = (L.g0 + gu) % 4
            dst = RAW[s][:, 0:L.kc * L.tpg * P].rearrange("p (k n) -> p k n", k=L.kc)
            if not isinstance(i, int):
                sp.wait_ge(lo_done, i * L.U + (L.n0 + (gu - 3) * L.tpg))
            elif L.g0 + i * L.gu + gu >= 4:
                sp.wait_ge(lo_done, group_end[L.g0 + i * L.gu + gu - 4])
            sp.dma_start(dst, L.src(i, gu, L.gu)).then_inc(raw_loaded[s], 16)
        for gu in range(min(L.gu, L.G)):
            one(0, gu)
        units(sp, min(L.gu, L.G), L.G, L.gu, one)

    def raw_tile(L, i, u):
        G = L.g0 + u // L.tpg
        v = RAW[G % 4][:, 0:L.kc * L.tpg * P].rearrange("p (k n) -> p k n", k=L.kc)
        h = u % L.tpg
        return G % 4, v[:, :, h * P:(h + 1) * P], i * (4 * L.gu) + 16 * (G // 4 + 1)

    def split_tile(W, L, u):
        o = (L.n0 + u) % L.slots * (DC if L.kc == DC else 24)
        return W[:, o * P:(o + L.kc) * P].rearrange("p (k n) -> p k n", k=L.kc)

    def hi_tile(act, L, i, u):
        n = i * L.U + (L.n0 + u)
        s, raw, landed = raw_tile(L, i, u)
        act.wait_ge(raw_loaded[s], landed)
        first = isinstance(i, int) and i * L.U + u < L.slots
        prev = layers[L.idx - 1] if first and L.idx else None
        if prev is not None and prev.slots != L.slots:
            act.wait_ge(mm_done, L.n0)
        else:
            paired = L.tok or (prev is not None and prev.tok)
            back = L.slots - 1 - (1 if paired and (L.n0 + u) % 2 == 0 else 0)
            if not isinstance(n, int) or n > back:
                act.wait_ge(mm_done, n - back)
        nc.scalar.activation(split_tile(WHI, L, u), raw, ACT.Copy).then_inc(hi_done, 1)

    def lo_tile(dve, L, i, u):
        _, raw, _ = raw_tile(L, i, u)
        dve.wait_ge(hi_done, i * L.U + (L.n0 + u + 1))
        nc.vector.tensor_tensor(split_tile(WLO, L, u), raw, split_tile(WHI, L, u).bitcast(f32),
                                ALU.subtract).then_inc(lo_done, 1)

    def run_layer(eng, L, make, work):
        nxt = layers[L.idx + 1] if L.idx + 1 < len(layers) else None
        if nxt is not None and nxt.name in fresh:
            nxt = None
        if L.name in fresh:
            for u in range(L.slots):
                make(eng, L, 0, u)

        def both(i, u):
            work(i, u)
            make(eng, L, i + (u + L.slots) // L.U, (u + L.slots) % L.U)
        units(eng, 0, L.T - L.slots, L.U, both)
        for m in range(L.T - L.slots, L.T):
            work(m // L.U, m % L.U)
            if nxt is not None and nxt.slots == L.slots:
                make(eng, nxt, 0, m + L.slots - L.T)
        if nxt is not None and nxt.slots != L.slots:
            for u in range(nxt.slots):
                make(eng, nxt, 0, u)

    def products(pe, L, xh, xl, behind=None):
        def one(i, u):
            n = i * L.U + (L.n0 + u)
            if not L.tok or u % 2 == 0:
                pe.wait_ge(lo_done, n + (2 if L.tok else 1))
            if not isinstance(n, int) or n >= 4:
                pe.wait_ge(evacuated, n - 3)
            if not L.tok:
                hi, lo = split_tile(WHI, L, u), split_tile(WLO, L, u)
                terms = [(w[:, k, :], x[:, k, :]) for k in range(L.kc)
                         for w, x in ((hi, xh), (hi, xl), (lo, xh))]
            else:
                tt, s = u % 2, (L.n0 + u) % 4 - u % 2
                wh, wl = (W[:, 0:32 * P].rearrange("p (s k n) -> p s k n", s=4, k=DC)[:, s:s + 2] for W in (WHI, WLO))
                terms = [(x[:, k, tt * P:(tt + 1) * P], w[:, :, k, :]) for k in range(DC)
                         for x, w in ((xh, wh), (xh, wl), (xl, wh))]
            o = bank[(L.n0 + u) % 4][:, 0:S]
            if L.tok:
                o = o.rearrange("p (a n) -> p a n", a=2)
            for j, (a, r) in enumerate(terms):
                last = nc.tensor.matmul(o, a, r, start=j == 0, stop=j == len(terms) - 1)
            last.then_inc(mm_done, 1)
            if behind is not None and (not isinstance(i, int) or i * L.U + u >= 2):
                behind(i + (u - 2) // L.U, (u - 2) % L.U)
        for u in range(min(4, L.T) if L.n0 == 0 else 0):
            one(0, u)
        start = 4 if L.n0 == 0 else 2 if behind is not None else 0
        for u in range(0 if L.n0 == 0 else start):
            one(0, u)
        units(pe, start, L.T, L.U, one)
        if behind is not None:
            for t in (L.T - 2, L.T - 1):
                behind(t // L.U, t % L.U)

    def tile_bank(L, u):
        return bank[(L.n0 + u) % 4][:, 0:S]

    def tile_end(L, i, u):
        return i * L.U + (L.n0 + u + 1)

    def chunk(t, j):
        if isinstance(j, int):
            return t[:, j, :]
        return t[:, ds(j, 1), :].rearrange("p a s -> p (a s)")

    def col(name, j=0):
        o = COL[name]
        if isinstance(j, int):
            return PRM[:, o + j:o + j + 1]
        return PRM[:, ds(j + o, 1)]

    act_f, vec = nc.scalar.activation, nc.vector
    TS, TTN, STT = vec.tensor_scalar, vec.tensor_tensor, vec.scalar_tensor_tensor

    class Norm:
        count = 0
        splits = 0

        def __init__(self, T, gain, shift=None, keep=False):
            self.k, self.T, self.gain, self.shift, self.keep = Norm.count, T, gain, shift, keep
            self.h = Norm.splits
            Norm.count += 1
            Norm.splits += 0 if keep else 1

        def act(self, act, own):
            k, T = self.k, self.T
            if k:
                act.wait_ge(sem("x_ready"), k)
            else:
                act.wait_ge(sem("x_loaded"), 16)
            for c in range(DC):
                act_f(T[:, c, :], XT[:, c, :], ACT.Square).then_inc(sem("squared"), 1)
            act.wait_ge(sem("mean_done"), k + 1)
            act_f(SD[:, :], bank[6][:, 0:S], ACT.Sqrt, bias=EPSC[:, 0:1]).then_inc(sem("root_done"), 1)
            for c in range(DC):
                act.wait_ge(sem("scaled"), DC * k + c + 1)
                f = act_f(T[:, c, :], T[:, c, :], ACT.Identity, scale=self.gain(c),
                          bias=self.shift(c) if self.shift else 0.0)
                if self.keep:
                    f.then_inc(sem("kept"), 1)
                else:
                    own.link(f)
                    act_f(HNH[:, c, :], T[:, c, :], ACT.Copy).then_inc(sem("hn_hi"), 1)

        def pe(self, pe):
            for c in range(DC):
                pe.wait_ge(sem("squared"), DC * self.k + c + 1)
                last = nc.tensor.matmul(bank[6][:, 0:S], MEAN[:, :], self.T[:, c, :], start=c == 0, stop=c == DC - 1)
            last.then_inc(sem("mean_done"), 1)

        def dve(self, dve, own):
            k, T = self.k, self.T
            dve.wait_ge(sem("root_done"), k + 1)
            own.link(vec.reciprocal(RS[:, :], SD[:, :]))
            for c in range(DC):
                TTN(T[:, c, :], XT[:, c, :], RS[:, :], ALU.mult).then_inc(sem("scaled"), 1)
            if not self.keep:
                for c in range(DC):
                    dve.wait_ge(sem("hn_hi"), DC * self.h + c + 1)
                    TTN(HNL[:, c, :], T[:, c, :], HNH[:, c, :].bitcast(f32), ALU.subtract).then_inc(sem("hn_lo"), 1)

        def wait(self, pe):
            pe.wait_ge(sem("hn_lo"), DC * (self.h + 1))

    programs = {"sp": [], "pool": [], "act": [], "dve": [], "pe": []}
    own = {}

    def phase(**parts):
        for name, f in parts.items():
            programs[name].append(f)
    ra = Region(work0)
    AW = [ra(f"AW{s}", [DC, D]) for s in range(2)]
    AROW = ra("AROW", [6, S])

    def setup_sp(sp):
        sp.dma_start(PRM[:, :], A["params"]).then_inc(sem("prm_loaded"), 16)
        sp.dma_start(SM[:, :], A["small"]).then_inc(sem("small_loaded"), 16)
        sp.dma_start(XT[:, :, :], A["xT"]).then_inc(sem("x_loaded"), 16)
        sp.dma_start(SINK[:, 0, :], A["sinks"]).then_inc(sem("sinks_loaded"), 16)
        aw = A["w_ada"][0].rearrange("(k p) n -> p k n", p=P)
        for r in range(6):
            if r >= 2:
                sp.wait_ge(sem("ada_mm"), r - 1)
            sp.dma_start(AW[r % 2][:, :, :], aw[:, :, D * r:D * (r + 1)]).then_inc(sem(f"aw_loaded{r % 2}"), 16)

    def setup_pool(pool):
        nc.gpsimd.memset(MEAN[:, :], 1.0 / D).then_inc(sem("filled"), 1)
        nc.gpsimd.memset(ONE[:, :], 1.0).then_inc(sem("filled"), 1)
        nc.gpsimd.memset(EPSC[:, :], EPS).then_inc(sem("filled"), 1)
        nc.gpsimd.memset(AROW[:, :, :], 0.0).then_inc(sem("filled"), 1)

    def setup_act(act):
        act.wait_ge(sem("filled"), 4)
        act.wait_ge(sem("prm_loaded"), 16)
        act_f(CSIL[:, :], PRM[:, COL["c"]:COL["c"] + DC], ACT.Silu).then_inc(sem("silu_c"), 1)
        for r in range(6):
            act.wait_ge(sem("ada_mm"), r + 1)
            for g in range(4):
                row = slice(32 * g, 32 * g + 1)
                act_f(AROW[row, r, :], bank[r][row, 0:S], ACT.Copy).then_inc(sem("ada_row"), 1)
        act.wait_ge(sem("ada_ready"), 5)

    def setup_pe(pe):
        pe.wait_ge(sem("filled"), 4)
        pe.wait_ge(sem("small_loaded"), 16)
        pe.wait_ge(sem("silu_c"), 1)
        def columns(r):
            pe.wait_ge(sem("ada_row"), 4 * r + 4)
            for c in range(DC):
                g = 32 * (c // 2)
                last = nc.tensor.matmul(bank[7][:, DC * r + c:DC * r + c + 1], AROW[:, r, (c % 2) * P:(c % 2 + 1) * P],
                                        IDENT[:, g:g + 1], start=True, stop=True)
            last.then_inc(sem("ada_col"), 1)
        for r in range(6):
            pe.wait_ge(sem(f"aw_loaded{r % 2}"), 16 * (r // 2 + 1))
            for k in range(DC):
                for g in range(4):
                    last = nc.tensor.matmul(bank[r][32 * g:32 * g + 1, 0:S], CSIL[:, k:k + 1],
                                            AW[r % 2][:, k, S * g:S * (g + 1)], start=k == 0, stop=k == DC - 1,
                                            tile_position=(0, 32 * g))
            last.then_inc(sem("ada_mm"), 1)
            if r >= 1:
                columns(r - 1)
        columns(5)

    def setup_dve(dve):
        dve.wait_ge(sem("prm_loaded"), 16)
        dve.wait_ge(sem("ada_col"), 6)
        TTN(ADA[:, :], bank[7][:, 0:48], PRM[:, COL["b_ada"]:COL["b_ada"] + 48], ALU.add).then_inc(sem("ada_ready"), 1)
        dve.wait_ge(sem("ada_ready"), 1)
        for r, (part, gain, plus) in enumerate(((1, "norm_pre_mix", 1.0), (2, "norm_post_mix", 0.0),
                                                (4, "norm_pre_ffn", 1.0), (5, "norm_post_ffn", 0.0))):
            STT(ADV[:, r, :], ADA[:, part * DC:(part + 1) * DC], plus,
                PRM[:, COL[gain]:COL[gain] + DC], ALU.add, ALU.mult).then_inc(sem("ada_ready"), 1)
        dve.wait_ge(sem("ada_ready"), 5)

    phase(sp=setup_sp, pool=setup_pool, act=setup_act, pe=setup_pe, dve=setup_dve)
    for L in layers:
        if L.name == "gate1_0" and "B" in phases:
            phase(sp=lambda sp: expert_loads(sp))
        phase(sp=lambda sp, L=L: load_layer(sp, L))
    if "B" in phases and "C" not in phases:
        phase(sp=lambda sp: expert_loads(sp))

    def bias_tables():
        rt = Region(work0)
        RB = rt("RB", [N_GROUPS * HEADS])
        OH = rt("OHB", [N_GROUPS, 384])
        RT = rt("RT", [N_GROUPS, 384])

        def pool(pool):
            pool.wait_ge(sem("ada_ready"), 5)
            pool.dma_start(RB[0:BUCKETS + 1, :], A["rel_bias_x"]).then_inc(sem("rb_loaded"), 16)
            pool.dma_start(OH[0:BUCKETS + 1, :, :], A["onehot"].rearrange("b (g j) -> b g j", g=N_GROUPS)).then_inc(sem("rb_loaded"), 16)
            pool.wait_ge(sem("rows_ready"), N_GROUPS)
            pool.dma_start(bias_rows.rearrange("g h j -> h g j"), RT[0:HEADS, :, :]).then_inc(sem("rows_stored"), 16)
            pool.wait_ge(sem("rows_stored"), 16)

        def pe(pe):
            pe.wait_ge(sem("rb_loaded"), 32)
            for g in range(N_GROUPS):
                nc.tensor.matmul(bank[g][0:HEADS, 0:384], RB[0:BUCKETS + 1, g * HEADS:(g + 1) * HEADS],
                                 OH[0:BUCKETS + 1, g, :], start=True, stop=True).then_inc(sem("rows_mm"), 1)

        def act(act):
            for g in range(N_GROUPS):
                act.wait_ge(sem("rows_mm"), g + 1)
                act_f(RT[0:HEADS, g, :], bank[g][0:HEADS, 0:384], ACT.Copy).then_inc(sem("rows_ready"), 1)
            act.wait_ge(sem("rows_stored"), 16)

        phase(pool=pool, pe=pe, act=act)

    if "D" in phases:
        bias_tables()

    def mixer():
        ra = Region(work0)
        PROJ = ra("PROJ", [44, S])
        XC = ra("XC", [DC, S])
        T1 = ra("T1", [DC, S])
        T2 = ra("T2", [DC, S])
        ya = ra.o
        YAH = ra("YAH", [DC, S], f32r)
        YAL = ra("YAL", [DC, S], f32r)
        rb = Region(ya)
        BDA, BDX = rb("BDA", [DC, P]), rb("BDX", [DC, P])
        T3 = rb("T3", [DC, S])
        rh = Region(hn0)
        YRH, YRL = rh("YRH", [DC, S], f32r), rh("YRL", [DC, S], f32r)
        rh = Region(hn0)
        MGH, MGL = rh("MGH", [DC, S], f32r), rh("MGL", [DC, S], f32r)
        ALB = Region(work0)("ALB", [HEADS, S])
        OF = Region(work0)("OF", [DC, S])
        rx = Region(work0 + 44 * KB)
        KD = rx("KD", [KV, S])
        VT = rx("VT", [TT, KV * HD])
        QS = rx("QS", [2, S])
        KS = rx("KS", [S])
        ES = [rx(f"AES{i}", [S]) for i in range(2)]
        ET = [rx(f"AET{i}", [S]) for i in range(2)]
        OT = rx("AOT", [TT, D])
        assert rx.o <= ya
        XR, GR, Q, K_, V_ = PROJ[:, 0:8, :], PROJ[:, 8:16, :], 16, 24, 26
        win, wor, woa, wout = (by_name[x] for x in ("win", "wor", "woa", "wout"))
        norm = Norm(T1, lambda c: ADV[:, 0, c:c + 1], lambda c: ADA[:, c:c + 1])

        def pool(pool):
            pool.wait_ge(sem("ada_ready"), 1)
            pool.dma_start(BDA[:, :, :], A["bd_a"]).then_inc(sem("bd_loaded"), 16)
            pool.dma_start(BDX[:, :, :], A["bd_x"]).then_inc(sem("bd_loaded"), 16)
            pool.wait_ge(sem("yr_lo"), 1)
            pool.dma_start(ALB[:, :, :], A["alibi"]).then_inc(sem("alibi_loaded"), 16)
            for j in range(KV):
                k = PROJ[64 * (j % 2):64 * (j % 2) + 64, K_ + j // 2, :]
                pool.dma_start(KD[0:64, j, :], k).then_inc(sem("kd_loaded"), 16)
                pool.dma_start(KD[64:128, j, :], k).then_inc(sem("kd_loaded"), 16)

        def evac_into(act, L, dst):
            def ev(i, u):
                act.wait_ge(mm_done, tile_end(L, i, u))
                act_f(chunk(dst, i * L.U + u), tile_bank(L, u), ACT.Copy).then_inc(evacuated, 1)
            return ev

        def act(act):
            o = own["act"]
            norm.act(act, o)
            act.wait_ge(sem("lam_abs"), 1)
            act_f(LAMV[:, 1, :], LAMV[:, 1, :], ACT.Exp, scale=-1.0).then_inc(sem("lam_exp"), 1)

            def ev_win(i, u):
                act.wait_ge(mm_done, tile_end(win, i, u))
                m = i * win.U + u
                act_f(chunk(PROJ, m), tile_bank(win, u), ACT.Identity, bias=col("b_in", m)).then_inc(evacuated, 1)
            run_layer(act, win, hi_tile, ev_win)
            for c in range(DC):
                act.wait_ge(sem("gates_mm"), c + 1)
                b = bank[4 + c % 2]
                o.mark(act_f(T1[:, c, :], b[:, 0:S], ACT.Sigmoid, bias=col("rg_b_a", c)))
                act_f(T2[:, c, :], b[:, S:2 * S], ACT.Sigmoid, bias=col("rg_b_x", c)).then_inc(sem("gates_out"), 1)
            o.wait()
            act.wait_ge(sem("lam_ready"), 1)
            for c in range(DC):
                act_f(T1[:, c, :], T1[:, c, :], ACT.Tanh, scale=LAMV[:, 4, c:c + 1]).then_inc(sem("half_tanh"), 1)
            act.wait_ge(sem("tanh_read"), 1)
            act_f(T1[:, :, :], T1[:, :, :], ACT.Sqrt).then_inc(sem("lru_root"), 1)
            act.wait_ge(sem("lru_in"), 1)
            act_f(T1[:, :, :], GR, ACT.Square).then_inc(sem("gelu_sq"), 1)
            act.wait_ge(sem("gelu_in"), 1)
            act_f(T1[:, :, :], T1[:, :, :], ACT.Tanh, scale=math.sqrt(2.0 / math.pi)).then_inc(sem("gelu_tanh"), 1)
            act.wait_ge(sem("y_rnn"), 1)
            act_f(YRH[:, :, :], T1[:, :, :], ACT.Copy).then_inc(sem("yr_hi"), 1)
            act.wait_ge(sem("v_T"), 1)
            act_f(VT[:, :, :], bank[4][:, :].rearrange("p (t n) -> p t n", t=TT), ACT.Copy).then_inc(sem("v_ready"), 1)
            with act.Fori(0, KV) as j:
                for u in range(8):
                    b = u % 2
                    n = (b + 1) * P
                    act.wait_ge(sem("a_max"), j * 8 + (u + 1))
                    act_f(ES[b][:, 0:n], bank[b][:, 0:n], ACT.Exp, bias=STAT[:, 0, b:b + 1],
                          accum_out=STAT[:, 1, b:b + 1]).then_inc(sem("a_exp"), 1)
                    act_f(STAT[:, 2, b:b + 1], SINK[:, 0, ds(j * 4 + u // 2, 1)], ACT.Exp,
                          bias=STAT[:, 0, b:b + 1]).then_inc(sem("a_sink"), 1)
            for m in range(4):
                act.wait_ge(sem("o_T"), m + 1)
                act_f(OF[:, 2 * m:2 * m + 2, :], bank[m][:, :].rearrange("p (a n) -> p a n", a=2),
                      ACT.Copy).then_inc(sem("o_full"), 1)
            act.wait_ge(sem("o_full"), 4)
            act_f(YAH[:, :, :], OF[:, :, :], ACT.Copy).then_inc(sem("ya_hi"), 1)
            act_f(PROJ[:, 28:44, :], PROJ[:, 28:44, :], ACT.Sigmoid).then_inc(sem("merge_gates"), 1)
            run_layer(act, wor, hi_tile, evac_into(act, wor, T2))
            run_layer(act, woa, hi_tile, evac_into(act, woa, T1))
            run_layer(act, wout, hi_tile, evac_into(act, wout, T1))
            act.wait_ge(evacuated, wout.n0 + 8)
            act_f(T2[:, :, :], T1[:, :, :], ACT.Square).then_inc(sem("post_sq"), 1)
            act.wait_ge(sem("post_mean"), 1)
            act_f(SD[:, :], bank[6][:, 0:S], ACT.Sqrt, bias=EPSC[:, 0:1]).then_inc(sem("post_root"), 1)

        def pe(pe):
            norm.pe(pe)
            norm.wait(pe)
            products(pe, win, HNH, HNL)
            pe.wait_ge(sem("bd_loaded"), 32)
            for c in range(DC):
                pe.wait_ge(sem("conv_done"), c + 1)
                if c >= 2:
                    pe.wait_ge(sem("gates_out"), c - 1)
                b = bank[4 + c % 2]
                nc.tensor.matmul(b[:, 0:S], BDA[:, c, :], XC[:, c, :], start=True, stop=True)
                nc.tensor.matmul(b[:, S:2 * S], BDX[:, c, :], XC[:, c, :], start=True, stop=True)\
                    .then_inc(sem("gates_mm"), 1)
            pe.wait_ge(sem("lru_in"), 1)
            for tt in range(TT):
                for m in range(2):
                    last = nc.tensor.transpose(bank[4][:, (2 * tt + m) * P:(2 * tt + m + 1) * P],
                                               PROJ[:, V_ + m, tt * P:(tt + 1) * P], IDENT)
            last.then_inc(sem("v_T"), 1)
            pe.wait_ge(sem("v_ready"), 1)
            pe.wait_ge(sem("alibi_loaded"), 16)
            with pe.Fori(0, KV) as j:
                def scores(u):
                    x, b = u // 2, u % 2
                    n = (b + 1) * P
                    h = slice(64 * (x % 2), 64 * (x % 2) + 64)
                    if u == 0:
                        pe.wait_ge(sem("a_staged"), j + 1)
                    if u >= 2:
                        pe.wait_ge(sem("a_exp"), j * 8 + (u - 1))
                    nc.tensor.matmul(bank[b][:, 0:n], QS[h, x // 2, b * P:(b + 1) * P], KS[h, 0:n], start=True, stop=False)
                    nc.tensor.matmul(bank[b][:, 0:n], IDENT, chunk(ALB, j * 4 + x)[:, S - n:S], start=False, stop=True)\
                        .then_inc(sem("a_scores"), 1)

                def weigh(u):
                    x, b = u // 2, u % 2
                    pe.wait_ge(sem("a_exp"), j * 8 + (u + 1))
                    for kb in range(b + 1):
                        last = nc.tensor.transpose(bank[2 + b][:, kb * P:(kb + 1) * P], ES[b][:, kb * P:(kb + 1) * P], IDENT)
                    last.then_inc(sem("a_T"), 1)
                    pe.wait_ge(sem("a_ET"), j * 8 + (u + 1))
                    if u >= 2:
                        pe.wait_ge(sem("a_out"), j * 8 + (u - 1))
                    for kb in range(b + 1):
                        last = nc.tensor.matmul(bank[4 + b][:, 0:HD], ET[b][:, kb * P:(kb + 1) * P],
                                                VT[:, kb, ds(j * HD, HD)], start=kb == 0, stop=kb == b)
                    last.then_inc(sem("a_pv"), 1)
                scores(0)
                for u in range(8):
                    if u < 7:
                        scores(u + 1)
                    weigh(u)
            pe.wait_ge(sem("a_out"), 8 * KV)
            for m in range(4):
                for c in range(2):
                    for tt in range(TT):
                        last = nc.tensor.transpose(bank[m][:, c * S + tt * P:c * S + (tt + 1) * P],
                                                   OT[:, tt, (2 * m + c) * P:(2 * m + c + 1) * P], IDENT)
                last.then_inc(sem("o_T"), 1)
            pe.wait_ge(sem("o_full"), 4)
            pe.wait_ge(sem("yr_lo"), 1)
            products(pe, wor, YRH, YRL)
            pe.wait_ge(sem("ya_lo"), 1)
            products(pe, woa, YAH, YAL)
            pe.wait_ge(sem("merged"), 8)
            products(pe, wout, MGH, MGL)
            pe.wait_ge(sem("post_sq"), 1)
            for c in range(DC):
                last = nc.tensor.matmul(bank[6][:, 0:S], MEAN[:, :], T2[:, c, :], start=c == 0, stop=c == DC - 1)
            last.then_inc(sem("post_mean"), 1)

        def dve(dve):
            o = own["dve"]
            norm.dve(dve, o)
            lam = PRM[:, COL["rg_lambda"]:COL["rg_lambda"] + DC]
            neg, e, z, z2, pz, den = (LAMV[:, r, :] for r in range(6))
            o.link(TS(neg, lam, -1.0, None, ALU.mult))
            TTN(e, neg, lam, ALU.max).then_inc(sem("lam_abs"), 1)
            dve.wait_ge(sem("lam_exp"), 1)
            o.link(TS(den, e, 2.0, None, ALU.add))
            o.link(vec.reciprocal(z2, den))
            o.link(TTN(z, e, z2, ALU.mult))
            o.link(TTN(z2, z, z, ALU.mult))
            o.link(vec.memset(pz, 1.0 / 17))
            for k in (15, 13, 11, 9, 7, 5, 3, 1):
                o.link(TTN(pz, pz, z2, ALU.mult))
                o.link(TS(pz, pz, 1.0 / k, None, ALU.add))
            o.link(STT(pz, pz, 2.0, z, ALU.mult, ALU.mult))
            o.link(TS(neg, neg, 0.0, None, ALU.max))
            o.link(TTN(pz, pz, neg, ALU.add))
            TS(pz, pz, 4.0, None, ALU.mult).then_inc(sem("lam_ready"), 1)
            dve.wait_ge(sem("sinks_loaded"), 16)
            o.link(TS(SINK[:, 1, :], SINK[:, 0, :], -1.0, None, ALU.mult))
            run_layer(dve, win, lo_tile, lambda i, u: None)
            dve.wait_ge(evacuated, win.n0 + 44)
            for c in range(DC):
                x, y = PROJ[:, c, :], XC[:, c, :]
                o.link(TS(y, x, col("conv_w", 3 * DC + c), col("conv_b", c), ALU.mult, ALU.add))
                for lag in (1, 2):
                    o.link(STT(y[:, lag:S], x[:, 0:S - lag], col("conv_w", (3 - lag) * DC + c), y[:, lag:S], ALU.mult, ALU.add))
                STT(y[:, 3:S], x[:, 0:S - 3], col("conv_w", c), y[:, 3:S], ALU.mult, ALU.add).then_inc(sem("conv_done"), 1)
            dve.wait_ge(sem("half_tanh"), DC)
            o.link(TS(T3[:, :, :], T1[:, :, :], 1.0, None, ALU.add))
            o.link(vec.reciprocal(XR, T3[:, :, :]))
            o.link(TTN(T3[:, :, :], T1[:, :, :], XR, ALU.mult))
            TTN(T3[:, :, :], XR, T3[:, :, :], ALU.subtract).then_inc(sem("tanh_read"), 1)
            o.link(TTN(T2[:, :, :], T2[:, :, :], XC[:, :, :], ALU.mult))
            dve.wait_ge(sem("lru_root"), 1)
            o.link(STT(T1[:, :, :], T1[:, :, :], 2.0, XR, ALU.mult, ALU.mult))
            o.link(vec.memset(T1[:, :, 0:1], 1.0))
            TTN(T2[:, :, :], T2[:, :, :], T1[:, :, :], ALU.mult).then_inc(sem("lru_in"), 1)
            dve.wait_ge(sem("lru_in"), 1)
            for c in range(DC):
                o.mark(vec.tensor_tensor_scan(XC[:, c, :], T3[:, c, :], T2[:, c, :], 0.0, ALU.mult, ALU.add))
            dve.wait_ge(sem("gelu_sq"), 1)
            o.link(TS(T1[:, :, :], T1[:, :, :], 0.044715, 1.0, ALU.mult, ALU.add))
            TTN(T1[:, :, :], T1[:, :, :], GR, ALU.mult).then_inc(sem("gelu_in"), 1)
            dve.wait_ge(sem("gelu_tanh"), 1)
            o.link(STT(T1[:, :, :], T1[:, :, :], 1.0, GR, ALU.add, ALU.mult))
            STT(T1[:, :, :], T1[:, :, :], 0.5, XC[:, :, :], ALU.mult, ALU.mult).then_inc(sem("y_rnn"), 1)
            o.link(TS(PROJ[:, Q:Q + 8, :], PROJ[:, Q:Q + 8, :], HD ** -0.5, None, ALU.mult))
            dve.wait_ge(sem("yr_hi"), 1)
            TTN(YRL[:, :, :], T1[:, :, :], YRH[:, :, :].bitcast(f32), ALU.subtract).then_inc(sem("yr_lo"), 1)
            dve.wait_ge(sem("yr_lo"), 1)
            dve.wait_ge(sem("v_ready"), 1)
            dve.wait_ge(sem("kd_loaded"), 16 * 2 * KV)
            with o.loop(0, KV, 1 + 8 * 3) as j:
                o.mark(vec.tensor_copy(QS[:, :, :], PROJ[:, ds(j * 2 + Q, 2), :]))
                vec.tensor_copy(KS[:, :], chunk(KD, j)).then_inc(sem("a_staged"), 1)

                def peak(u):
                    x, b = u // 2, u % 2
                    n = (b + 1) * P
                    if u >= 2:
                        dve.wait_ge(sem("a_sink"), j * 8 + (u - 1))
                    dve.wait_ge(sem("a_scores"), j * 8 + (u + 1))
                    m = STAT[:, 0, b:b + 1]
                    o.link(vec.tensor_reduce(m, bank[b][:, 0:n], AX.X, ALU.max, negate=True))
                    TTN(m, m, SINK[:, 1, ds(j * 4 + x, 1)], ALU.min).then_inc(sem("a_max"), 1)

                def weigh(u):
                    x, b = u // 2, u % 2
                    n = (b + 1) * P
                    dve.wait_ge(sem("a_T"), j * 8 + (u + 1))
                    vec.tensor_copy(ET[b][:, 0:n], bank[2 + b][:, 0:n]).then_inc(sem("a_ET"), 1)
                    dve.wait_ge(sem("a_sink"), j * 8 + (u + 1))
                    o.link(TTN(STAT[:, 3, b:b + 1], STAT[:, 1, b:b + 1], STAT[:, 2, b:b + 1], ALU.add))
                    o.link(vec.reciprocal(STAT[:, 4, b:b + 1], STAT[:, 3, b:b + 1]))
                    dve.wait_ge(sem("a_pv"), j * 8 + (u + 1))
                    TS(OT[:, b, ds(j * 256 + x * HD, HD)], bank[4 + b][:, 0:HD], STAT[:, 4, b:b + 1], None,
                       ALU.mult).then_inc(sem("a_out"), 1)
                peak(0)
                for u in range(8):
                    if u < 7:
                        peak(u + 1)
                    weigh(u)
            dve.wait_ge(sem("ya_hi"), 1)
            TTN(YAL[:, :, :], OF[:, :, :], YAH[:, :, :].bitcast(f32), ALU.subtract).then_inc(sem("ya_lo"), 1)

            def post_wor(i, u):
                m = i * wor.U + u
                dve.wait_ge(evacuated, tile_end(wor, i, u))
                o.mark(TTN(T2[:, m, :], T2[:, m, :], PROJ[:, 28 + m, :], ALU.mult))

            def post_woa(i, u):
                m = i * woa.U + u
                dve.wait_ge(evacuated, tile_end(woa, i, u))
                o.link(TTN(T1[:, m, :], T1[:, m, :], PROJ[:, 36 + m, :], ALU.mult))
                o.link(TTN(T1[:, m, :], T1[:, m, :], T2[:, m, :], ALU.add))
                o.link(vec.tensor_copy(MGH[:, m, :], T1[:, m, :]))
                TTN(MGL[:, m, :], T1[:, m, :], MGH[:, m, :].bitcast(f32), ALU.subtract).then_inc(sem("merged"), 1)
            dve.wait_ge(sem("merge_gates"), 1)
            run_layer(dve, wor, lo_tile, post_wor)
            dve.wait_ge(mm_done, wor.n0 + 8)
            run_layer(dve, woa, lo_tile, post_woa)
            run_layer(dve, wout, lo_tile, lambda i, u: None)
            dve.wait_ge(sem("post_root"), 1)
            o.link(vec.reciprocal(RS[:, :], SD[:, :]))
            for c in range(DC):
                o.link(TTN(T1[:, c, :], T1[:, c, :], RS[:, :], ALU.mult))
                last = STT(XT[:, c, :], T1[:, c, :], ADV[:, 1, c:c + 1], XT[:, c, :], ALU.mult, ALU.add)
                if c < DC - 1:
                    o.mark(last)
            last.then_inc(sem("x_ready"), 1)

        phase(pool=pool, act=act, pe=pe, dve=dve)

    if "A" in phases:
        mixer()
    rw = Region(body0)
    W1 = rw("W1", [4, 2, 2 * FF])
    assert rw.o <= work0
    rw = Region(work0)
    W2 = rw("W2", [2, 4, D])
    B1 = rw("B1", [2 * FF])
    H2K = rw("H2K", [TT, D])
    ACC = rw("ACC", [TT, D])
    H2F = rw("H2F", [DC, S])
    PSEL = rw("PSEL", [TT, SLOTS])
    PGAT = rw("PGAT", [TT, 2 * SLOTS])
    PGT = rw("PGT", [S])
    XG = rw("XG", [DC, SLOTS])
    small_at = rw.o
    GLU = rw("GLU", [2, S])
    LIN = rw("LIN", [2, S])
    SIG = rw("SIG", [2, S])
    AC = rw("AC", [4, P])
    AT = rw("AT", [4, P])
    YE = rw("YE", [512])
    NBI = rw("NBI", [3 * NE], i32)
    RANK = rw("RANK", [TT, NE])
    GAT = rw("GAT", [TT, NE])
    RKE = rw("RKE", [TT])
    GTE = rw("GTE", [TT])
    rs = Region(small_at)
    B2A = rs("B2A", [D])
    RTW = rs("RTW", [DC, NE])
    RTB = rs("RTB", [NE])
    IOE = rs("IOE", [NE])
    LG = rs("LG", [TT, NE])
    TOPV = rs("TOPV", [TT, 8])
    TOPI = rs("TOPI", [TT, 8], u32)
    TOPF = rs("TOPF", [TT, 8])
    EXV = rs("EXV", [TT, TOPK])
    GSC = rs("GSC", [8])
    MSK = rs("MSK", [TT, NE])
    ONEH = rs("ONEH", [TT, NE])
    NBF = rs("NBF", [6, NE])
    GTT = rs("GTT", [S])
    assert rs.o <= small_at + 12 * KB

    class Blocks:

        def __init__(self, eng, name):
            self.eng, self.reg = eng, eng.alloc_register(f"blocks_{name}")
            eng.reg_mov(self.reg, 1)

        def now(self):
            return self.eng.snap(self.reg, min_val=1, max_val=S // SLOTS * NE)

        def end(self):
            self.eng.reg_add(self.reg, self.reg, 1)

        def of(self, e):
            return self.eng.value_load(NBI[0:1, ds(e, 1)], min_val=1, max_val=S // SLOTS)

    def expert_loads(sp):
        w1 = A["moe_w1"][0].rearrange("e (q k p) n -> e q p k n", q=4, p=P)
        w2 = A["moe_w2"][0].rearrange("e (q k p) n -> e q p k n", q=2, p=P)
        b1 = A["moe_b1"][0]

        def load(e, mm1_free=None, mm2_free=None):
            def at_e(w, q):
                if isinstance(e, int):
                    return w[e, q]
                return w[ds(e, 1), q].rearrange("a p k n -> (a p) k n")
            if mm1_free is not None:
                sp.wait_ge(sem("mm1_done"), mm1_free)
            sp.dma_start(B1[0:1, :], b1[e:e + 1, :] if isinstance(e, int) else b1[ds(e, 1), :])\
                .then_inc(sem("b1_loaded"), 16)
            for q in range(4):
                if mm1_free is not None:
                    sp.wait_ge(sem("mm1_done"), mm1_free + q)
                sp.dma_start(W1[:, q], at_e(w1, q)).then_inc(sem(f"w1_loaded{q}"), 16)
            for q in range(2):
                if mm2_free is not None:
                    sp.wait_ge(sem("mm2_done"), mm2_free + q)
                sp.dma_start(W2[:, q], at_e(w2, q)).then_inc(sem(f"w2_loaded{q}"), 16)
        if "A" in phases:
            sp.wait_ge(mm_done, by_name["wout"].n0 + 8)
        else:
            sp.wait_ge(sem("ada_ready"), 5)
        load(0)
        sp.wait_ge(sem("blocks_ready"), 1)
        with sp.Fori(1, NE) as e:
            f1 = sp.value_load(NBI[0:1, ds(e + (NE - 1), 1)], min_val=1, max_val=4 * S // SLOTS * NE)
            f2 = sp.value_load(NBI[0:1, ds(e + (2 * NE - 1), 1)], min_val=1, max_val=2 * S // SLOTS * NE)
            load(e, f1, f2)

    def experts():
        norm = Norm(H2F, lambda c: ADV[:, 2, c:c + 1], lambda c: ADA[:, 24 + c:25 + c], keep=True)
        kx = norm.k

        def pool(pool):
            if kx:
                pool.wait_ge(sem("x_ready"), kx)
            else:
                pool.wait_ge(sem("ada_ready"), 5)
            pool.dma_start(RTW[:, :, :], A["router_w"]).then_inc(sem("router_loaded"), 16)
            pool.dma_start(RTB[:, :], A["router_b"]).then_inc(sem("router_loaded"), 16)
            pool.dma_start(B2A[0:NE, :], A["moe_b2"][0]).then_inc(sem("router_loaded"), 16)
            pool.dma_start(IOE[:, :], A["expert_no"]).then_inc(sem("router_loaded"), 16)

        def act(act):
            o = own["act"]
            norm.act(act, o)
            for m in range(4):
                act.wait_ge(sem("h_T"), m + 1)
                act_f(H2K[:, m // 2, 512 * (m % 2):512 * (m % 2 + 1)], bank[m][:, :], ACT.Copy).then_inc(sem("h_ready"), 1)
            for tt in range(TT):
                act.wait_ge(sem("top_ready"), tt + 1)
                act_f(EXV[:, tt, :], TOPV[:, tt, 0:TOPK], ACT.Exp, bias=GSC[:, tt:tt + 1],
                      accum_out=GSC[:, 2 + tt:3 + tt]).then_inc(sem("top_exp"), 1)
            act.wait_ge(sem("gates_T"), 1)
            act_f(GTT[0:NE, :], bank[7][0:NE, 0:S], ACT.Copy).then_inc(sem("gt_ready"), 1)
            for m in range(4):
                act.wait_ge(sem("b2_mm"), m + 1)
                act_f(ACC[:, m // 2, 512 * (m % 2):512 * (m % 2 + 1)], bank[m][:, :], ACT.Copy).then_inc(sem("acc_ready"), 1)
            blocks = Blocks(act, "act")
            act.wait_ge(sem("blocks_ready"), 1)
            with act.Fori(0, NE) as e:
                with act.Fori(0, blocks.of(e)):
                    d = blocks.now()
                    act.wait_ge(sem("xg_mm"), d)
                    act_f(XG[:, :, :], bank[4][:, :].rearrange("p (k s) -> p k s", k=DC), ACT.Copy).then_inc(sem("xg_ready"), 1)
                    act.wait_ge(sem("glu_ready"), d)
                    act_f(SIG[:, :, :], GLU[:, :, :], ACT.Sigmoid, scale=1.702).then_inc(sem("sig_ready"), 1)
                    act.wait_ge(sem("at_mm"), d)
                    act_f(AT[:, :, :], bank[5][:, :].rearrange("p (k s) -> p k s", k=4), ACT.Copy).then_inc(sem("at_ready"), 1)
                    act.wait_ge(sem("mm2_done"), d * 2)
                    act_f(YE[:, :], bank[6][:, :], ACT.Copy).then_inc(sem("y_ready"), 1)
                    blocks.end()
            act.wait_ge(sem("acc_done"), 1)
            for tt in range(TT):
                act_f(H2F[:, 4 * tt:4 * tt + 4, :], ACC[:, tt, :].rearrange("p (a s) -> p a s", a=4), ACT.Square,
                      accum_out=STAT[:, 5, tt:tt + 1]).then_inc(sem("ff_sq"), 1)
            act.wait_ge(sem("ff_sq"), 2)
            act_f(STAT[:, 6, :], STAT[:, 5, :], ACT.Sqrt, scale=1.0 / D, bias=EPSC[:, 0:1]).then_inc(sem("ff_root"), 1)

        def pe(pe):
            norm.pe(pe)
            pe.wait_ge(sem("kept"), DC)
            for m in range(4):
                for c in range(4):
                    k = 4 * (m % 2) + c
                    last = nc.tensor.transpose(bank[m][:, c * P:(c + 1) * P],
                                               H2F[:, k, (m // 2) * P:(m // 2 + 1) * P], IDENT)
                last.then_inc(sem("h_T"), 1)
            pe.wait_ge(sem("router_loaded"), 64)
            for tt in range(TT):
                for k in range(DC):
                    last = nc.tensor.matmul(bank[4][:, tt * NE:(tt + 1) * NE], H2F[:, k, tt * P:(tt + 1) * P],
                                            RTW[:, k, :], start=k == 0, stop=k == DC - 1)
            last.then_inc(sem("logits_mm"), 1)
            pe.wait_ge(sem("mask_ready"), 1)
            nc.tensor.matmul(bank[5][:, 0:NE], BEFORE, MSK[:, 0, :], start=True, stop=True)
            nc.tensor.matmul(bank[5][:, NE:2 * NE], BEFORE, MSK[:, 1, :], start=True, stop=False)
            nc.tensor.matmul(bank[5][:, NE:2 * NE], ONE[:, :], MSK[:, 0, :], start=False, stop=True).then_inc(sem("rank_mm"), 1)
            nc.tensor.matmul(bank[6][0:1, 0:NE], ONE[:, 0:1], MSK[:, 0, :], start=True, stop=False)
            nc.tensor.matmul(bank[6][0:1, 0:NE], ONE[:, 0:1], MSK[:, 1, :], start=False, stop=True).then_inc(sem("count_mm"), 1)
            pe.wait_ge(sem("gat_ready"), 1)
            for tt in range(TT):
                last = nc.tensor.transpose(bank[7][0:NE, tt * P:(tt + 1) * P], GAT[:, tt, :], IDENT)
            last.then_inc(sem("gates_T"), 1)
            pe.wait_ge(sem("gt_ready"), 1)
            pe.wait_ge(sem("h_ready"), 4)
            for m in range(4):
                nc.tensor.matmul(bank[m][:, :], GTT[0:NE, (m // 2) * P:(m // 2 + 1) * P],
                                 B2A[0:NE, 512 * (m % 2):512 * (m % 2 + 1)], start=True, stop=True).then_inc(sem("b2_mm"), 1)
            pe.wait_ge(sem("acc_ready"), 4)
            blocks = Blocks(pe, "pe")
            pe.wait_ge(sem("blocks_ready"), 1)
            with pe.Fori(0, NE) as e:
                with pe.Fori(0, blocks.of(e)):
                    d = blocks.now()
                    pe.wait_ge(sem("p_ready"), d)
                    for tt in range(TT):
                        last = nc.tensor.transpose(bank[7][:, tt * P:(tt + 1) * P], PGAT[:, tt, :], IDENT)
                    last.then_inc(sem("pgt_mm"), 1)
                    for k in range(DC):
                        for tt in range(TT):
                            last = nc.tensor.matmul(bank[4][:, k * SLOTS:(k + 1) * SLOTS], H2K[:, tt, k * P:(k + 1) * P],
                                                    PSEL[:, tt, :], start=tt == 0, stop=tt == TT - 1)
                    last.then_inc(sem("xg_mm"), 1)
                    pe.wait_ge(sem("b1_loaded"), e * 16 + 16)
                    for j in range(2):
                        for g in range(2):
                            nc.tensor.matmul(bank[j][64 * g:64 * g + 64, :], ONE[0:1, 0:SLOTS],
                                             B1[0:1, 1024 * g + 512 * j:1024 * g + 512 * (j + 1)], start=True, stop=False)
                    pe.wait_ge(sem("xg_ready"), d)
                    for q in range(4):
                        pe.wait_ge(sem(f"w1_loaded{q}"), e * 16 + 16)
                        for k in range(2):
                            for j in range(2):
                                for g in range(2):
                                    last = nc.tensor.matmul(bank[j][64 * g:64 * g + 64, :], XG[:, 2 * q + k, :],
                                                            W1[:, q, k, 1024 * g + 512 * j:1024 * g + 512 * (j + 1)],
                                                            start=False, stop=q == 3 and k == 1)
                        last.then_inc(sem("mm1_done"), 1)
                    pe.wait_ge(sem("ac_ready"), d)
                    for b in range(4):
                        last = nc.tensor.transpose(bank[5][:, b * P:(b + 1) * P], AC[:, b, :], IDENT)
                    last.then_inc(sem("at_mm"), 1)
                    pe.wait_ge(sem("at_ready"), d)
                    for q in range(2):
                        pe.wait_ge(sem(f"w2_loaded{q}"), e * 16 + 16)
                        for b in range(4):
                            for g in range(2):
                                last = nc.tensor.matmul(bank[6][64 * g:64 * g + 64, :], AT[:, b, 64 * q:64 * q + 64],
                                                        W2[:, q, b, 512 * g:512 * (g + 1)],
                                                        start=q == 0 and b == 0, stop=q == 1 and b == 3)
                        last.then_inc(sem("mm2_done"), 1)
                    pe.wait_ge(sem("pgt_ready"), d)
                    pe.wait_ge(sem("y_ready"), d)
                    for m in range(4):
                        tt, g = m // 2, m % 2
                        if m >= 2:
                            pe.wait_ge(sem("added"), d * 4 - (5 - m))
                        nc.tensor.matmul(bank[2 + g][:, :], PGT[64 * g:64 * g + 64, tt * P:(tt + 1) * P],
                                         YE[64 * g:64 * g + 64, :], start=True, stop=True).then_inc(sem("comb_mm"), 1)
                    blocks.end()
            pe.wait_ge(sem("ff_scaled"), 2)
            for m in range(4):
                for c in range(2):
                    for tt in range(TT):
                        last = nc.tensor.transpose(bank[m][:, c * S + tt * P:c * S + (tt + 1) * P],
                                                   ACC[:, tt, (2 * m + c) * P:(2 * m + c + 1) * P], IDENT)
                last.then_inc(sem("ff_T"), 1)

        def dve(dve):
            o = own["dve"]
            norm.dve(dve, o)
            dve.wait_ge(sem("router_loaded"), 64)
            dve.wait_ge(sem("logits_mm"), 1)
            for tt in range(TT):
                o.link(TTN(LG[:, tt, :], bank[4][:, tt * NE:(tt + 1) * NE], RTB[:, :], ALU.add))
                o.link(vec.max(TOPV[:, tt, :], LG[:, tt, :]))
                o.mark(vec.max_index(TOPI[:, tt, :], TOPV[:, tt, :], LG[:, tt, :]))
                TS(GSC[:, tt:tt + 1], TOPV[:, tt, 0:1], -1.0, None, ALU.mult).then_inc(sem("top_ready"), 1)
            o.wait()
            for tt in range(TT):
                o.link(vec.tensor_copy(TOPF[:, tt, :], TOPI[:, tt, :]))
                dve.wait_ge(sem("top_exp"), tt + 1)
                o.link(vec.reciprocal(GSC[:, 4 + tt:5 + tt], GSC[:, 2 + tt:3 + tt]))
                o.link(TS(EXV[:, tt, :], EXV[:, tt, :], GSC[:, 4 + tt:5 + tt], None, ALU.mult))
                for k in range(TOPK):
                    first = k == 0
                    o.link(TS(ONEH[:, tt, :], IOE[:, :], TOPF[:, tt, k:k + 1], None, ALU.is_equal))
                    if first:
                        o.mark(vec.tensor_copy(MSK[:, tt, :], ONEH[:, tt, :]))
                        o.link(TS(GAT[:, tt, :], ONEH[:, tt, :], EXV[:, tt, 0:1], None, ALU.mult))
                    else:
                        o.mark(TTN(MSK[:, tt, :], MSK[:, tt, :], ONEH[:, tt, :], ALU.add))
                        o.link(STT(GAT[:, tt, :], ONEH[:, tt, :], EXV[:, tt, k:k + 1], GAT[:, tt, :], ALU.mult, ALU.add))
            TS(ONEH[:, :, :], MSK[:, :, :], 4096.0, -4096.0, ALU.mult, ALU.add).then_inc(sem("mask_ready"), 1)
            dve.wait_ge(sem("mask_ready"), 1)
            dve.wait_ge(sem("rank_mm"), 1)
            TTN(RANK[:, :, :], bank[5][:, 0:TT * NE].rearrange("p (t e) -> p t e", t=TT), ONEH[:, :, :],
                ALU.add).then_inc(sem("gat_ready"), 1)
            dve.wait_ge(sem("count_mm"), 1)
            cnt = NBF[0:1, 0, :]
            o.link(vec.tensor_copy(cnt, bank[6][0:1, 0:NE]))
            o.link(TS(NBF[0:1, 1, :], cnt, float(SLOTS), 1.0, ALU.is_gt, ALU.add))
            for b in range(2, S // SLOTS):
                o.link(TS(NBF[0:1, 2, :], cnt, float(b * SLOTS), None, ALU.is_gt))
                o.link(TTN(NBF[0:1, 1, :], NBF[0:1, 1, :], NBF[0:1, 2, :], ALU.add))
            o.link(vec.memset(NBF[0:1, 2, :], 1.0))
            o.link(vec.tensor_tensor_scan(NBF[0:1, 5, :], NBF[0:1, 2, :], NBF[0:1, 1, :], 0.0, ALU.mult, ALU.add))
            o.link(TS(NBF[0:1, 2, :], NBF[0:1, 5, :], 4.0, -3.0, ALU.mult, ALU.add))
            o.link(TS(NBF[0:1, 3, :], NBF[0:1, 5, :], 2.0, -1.0, ALU.mult, ALU.add))
            vec.tensor_copy(NBI[0:1, :], NBF[0:1, 1:4, :].rearrange("p a e -> p (a e)")).then_inc(sem("blocks_ready"), 1)
            dve.wait_ge(sem("blocks_ready"), 1)
            dve.wait_ge(sem("acc_ready"), 4)
            blocks = Blocks(dve, "dve")
            with dve.Fori(0, NE) as e:
                vec.tensor_copy(RKE[:, :], RANK[:, :, ds(e, 1)].rearrange("p t a -> p (t a)"))
                vec.tensor_copy(GTE[:, :], GAT[:, :, ds(e, 1)].rearrange("p t a -> p (t a)")).then_inc(sem("e_taken"), 1)
                dve.wait_ge(sem("e_taken"), e + 1)
                with dve.Fori(0, blocks.of(e)):
                    d = blocks.now()
                    for tt in range(TT):
                        TS(PSEL[:, tt, :], SLOT[:, 0:SLOTS], RKE[:, tt:tt + 1], None, ALU.is_equal)
                        last = TS(PGAT[:, tt, :], SLOT[:, :], RKE[:, tt:tt + 1], GTE[:, tt:tt + 1], ALU.is_equal, ALU.mult)
                    last.then_inc(sem("p_ready"), 1)
                    dve.wait_ge(sem("pgt_mm"), d)
                    vec.tensor_copy(PGT[:, :], bank[7][:, 0:S]).then_inc(sem("pgt_ready"), 1)
                    TS(RKE[:, :], RKE[:, :], -float(SLOTS), None, ALU.add).then_inc(sem("rk_next"), 1)
                    dve.wait_ge(sem("mm1_done"), d * 4)
                    pairs = [bank[j][:, :].rearrange("p (n a) -> p n a", a=2) for j in range(2)]
                    for j in range(2):
                        last = TS(GLU[:, j, :], pairs[j][:, :, 0], 7.0, None, ALU.min)
                    last.then_inc(sem("glu_ready"), 1)
                    for j in range(2):
                        last = TS(LIN[:, j, :], pairs[j][:, :, 1], -7.0, 7.0, ALU.max, ALU.min)
                    last.then_inc(sem("lin_ready"), 1)
                    dve.wait_ge(sem("lin_ready"), d)
                    STT(LIN[:, :, :], LIN[:, :, :], 1.0, GLU[:, :, :], ALU.add, ALU.mult).then_inc(sem("lin_glu"), 1)
                    dve.wait_ge(sem("lin_glu"), d)
                    dve.wait_ge(sem("sig_ready"), d)
                    TTN(AC[:, :, :].rearrange("p a b -> p (a b)"), LIN[:, :, :].rearrange("p a b -> p (a b)"),
                        SIG[:, :, :].rearrange("p a b -> p (a b)"), ALU.mult).then_inc(sem("ac_ready"), 1)
                    for m in range(4):
                        tt, g = m // 2, m % 2
                        dve.wait_ge(sem("comb_mm"), d * 4 + (m - 3))
                        a = ACC[:, tt, 512 * g:512 * (g + 1)]
                        TTN(a, a, bank[2 + g][:, :], ALU.add).then_inc(sem("added"), 1)
                    dve.wait_ge(sem("added"), d * 4)
                    dve.wait_ge(sem("rk_next"), d)
                    blocks.end()
            vec.memset(STAT[:, 5, :], 0.0).then_inc(sem("acc_done"), 1)
            dve.wait_ge(sem("ff_root"), 1)
            o.link(vec.reciprocal(STAT[:, 7, :], STAT[:, 6, :]))
            for tt in range(TT):
                TS(ACC[:, tt, :], ACC[:, tt, :], STAT[:, 7, tt:tt + 1], None, ALU.mult).then_inc(sem("ff_scaled"), 1)
            for c in range(DC):
                dve.wait_ge(sem("ff_T"), c // 2 + 1)
                last = STT(XT[:, c, :], bank[c // 2][:, (c % 2) * S:(c % 2 + 1) * S], ADV[:, 3, c:c + 1], XT[:, c, :],
                           ALU.mult, ALU.add)
            last.then_inc(sem("x_ready"), 1)
        phase(pool=pool, act=act, pe=pe, dve=dve)

    if "B" in phases:
        experts()
    XN = Region(work0)("XN", [DC, S])

    def split_into(o, dst_hi, dst_lo, src, name):
        o.link(vec.tensor_copy(dst_hi, src))
        TTN(dst_lo, src, dst_hi.bitcast(f32), ALU.subtract).then_inc(sem(name), 1)

    ffn_count = [0]

    def ffn(tag, gain, row):
        rg = Region(work0)
        GATE = rg(f"GATE{tag}", [FC, S])
        MIH = rg(f"MIH{tag}", [FC, S], f32r)
        MIL = rg(f"MIL{tag}", [FC, S], f32r)
        UP = rg(f"UP{tag}", [4, S])
        DX = rg(f"DX{tag}", [DC, S])
        gate, up, down = (by_name[f"{x}{tag}"] for x in ("gate", "up", "down"))
        norm = Norm(XN, lambda c: col(gain, row * DC + c))
        turn = ffn_count[0]
        ffn_count[0] += 1

        def act(act):
            norm.act(act, own["act"])

            def ev_gate(i, u):
                act.wait_ge(mm_done, tile_end(gate, i, u))
                act_f(chunk(GATE, i * gate.U + u), tile_bank(gate, u), ACT.Silu).then_inc(evacuated, 1)

            def ev_up(i, u):
                act.wait_ge(mm_done, tile_end(up, i, u))
                act_f(UP[:, u % 4, :], tile_bank(up, u), ACT.Copy).then_inc(evacuated, 1)

            def ev_down(i, u):
                act.wait_ge(mm_done, tile_end(down, i, u))
                act_f(chunk(DX, i * down.U + u), tile_bank(down, u), ACT.Copy, scale=0.5).then_inc(evacuated, 1)
            run_layer(act, gate, hi_tile, ev_gate)
            run_layer(act, up, hi_tile, ev_up)
            run_layer(act, down, hi_tile, ev_down)

        def pe(pe):
            norm.pe(pe)
            norm.wait(pe)
            products(pe, gate, HNH, HNL)
            products(pe, up, HNH, HNL)
            pe.wait_ge(sem("mid_done"), (turn + 1) * FC)
            products(pe, down, MIH, MIL)

        def dve(dve):
            o = own["dve"]
            norm.dve(dve, o)

            def post_up(i, u):
                dve.wait_ge(evacuated, tile_end(up, i, u))
                m = i * up.U + u
                g = chunk(GATE, m)
                TTN(g, g, UP[:, u % 4, :], ALU.mult).then_inc(sem("mid_mult"), 1)
                dve.wait_ge(sem("mid_mult"), turn * FC + m + 1)
                vec.tensor_copy(chunk(MIH, m), g).then_inc(sem("mid_hi"), 1)
                dve.wait_ge(sem("mid_hi"), turn * FC + m + 1)
                TTN(chunk(MIL, m), g, chunk(MIH, m).bitcast(f32), ALU.subtract).then_inc(sem("mid_done"), 1)

            def post_down(i, u):
                m = i * down.U + u
                dve.wait_ge(evacuated, tile_end(down, i, u))
                x = chunk(XT, m)
                TTN(x, x, chunk(DX, m), ALU.add).then_inc(sem("added_x"), 1)
            run_layer(dve, gate, lo_tile, lambda i, u: None)
            run_layer(dve, up, lo_tile, post_up)
            run_layer(dve, down, lo_tile, post_down)
            dve.wait_ge(sem("added_x"), residuals.next_total())
            vec.memset(STAT[:, 6, :], 0.0).then_inc(sem("x_ready"), 1)
        phase(act=act, pe=pe, dve=dve)

    class Residuals:
        total = 0

        def next_total(self):
            self.total += DC
            return self.total
    residuals = Residuals()

    def conv_mixer():
        rg = Region(work0)
        C = rg("CC", [DC, S])
        VP = rg("VP", [DC, S + 2])
        B = rg("CB", [DC, S])
        CT = rg("CT", [DC, S])
        OH, OL = rg("COH", [DC, S], f32r), rg("COL", [DC, S], f32r)
        DX = rg("DXC", [DC, S])
        U_ = rg("CUU", [4, S])
        cu, cb, co = (by_name[x] for x in ("conv_cu", "conv_b", "conv_out"))
        norm = Norm(XN, lambda c: col("norm_mix_2", c))

        def act(act):
            norm.act(act, own["act"])

            def ev_cu(i, u):
                m = i * cu.U + u
                act.wait_ge(mm_done, tile_end(cu, i, u))
                if m >= 12:
                    act.wait_ge(sem("cv_in"), m - 11)
                dst = C[:, m, :] if m < DC else U_[:, m % 4, :]
                act_f(dst, tile_bank(cu, u), ACT.Copy).then_inc(evacuated, 1)

            def ev(L, dst):
                def f(i, u):
                    act.wait_ge(mm_done, tile_end(L, i, u))
                    act_f(dst[:, i * L.U + u, :], tile_bank(L, u), ACT.Copy).then_inc(evacuated, 1)
                return f
            run_layer(act, cu, hi_tile, ev_cu)
            run_layer(act, cb, hi_tile, ev(cb, B))
            run_layer(act, co, hi_tile, ev(co, DX))

        def pe(pe):
            norm.pe(pe)
            norm.wait(pe)
            products(pe, cu, HNH, HNL)
            products(pe, cb, HNH, HNL)
            pe.wait_ge(sem("conv_split"), DC)
            products(pe, co, OH, OL)

        def dve(dve):
            o = own["dve"]
            norm.dve(dve, o)

            def post_cu(i, u):
                m = i * cu.U + u - DC
                if m < 0:
                    return
                dve.wait_ge(evacuated, tile_end(cu, i, u))
                if m == 0:
                    o.link(vec.memset(VP[:, :, 0:2], 0.0))
                v = VP[:, m, :]
                TTN(v[:, 2:S + 2], C[:, m, :], U_[:, m % 4, :], ALU.mult).then_inc(sem("cv_in"), 1)
                dve.wait_ge(sem("cv_in"), m + 1)
                w = [col("conv_w_2", lag * DC + m) for lag in range(CONV_W2)]
                o.link(TS(CT[:, m, :], v[:, 2:S + 2], w[0], None, ALU.mult))
                o.link(STT(CT[:, m, :], v[:, 1:S + 1], w[1], CT[:, m, :], ALU.mult, ALU.add))
                o.link(STT(CT[:, m, :], v[:, 0:S], w[2], CT[:, m, :], ALU.mult, ALU.add))

            def post_b(i, u):
                m = i * cb.U + u
                dve.wait_ge(evacuated, tile_end(cb, i, u))
                o.link(TTN(CT[:, m, :], CT[:, m, :], B[:, m, :], ALU.mult))
                split_into(o, OH[:, m, :], OL[:, m, :], CT[:, m, :], "conv_split")

            def post_out(i, u):
                m = i * co.U + u
                dve.wait_ge(evacuated, tile_end(co, i, u))
                TTN(XT[:, m, :], XT[:, m, :], DX[:, m, :], ALU.add).then_inc(sem("added_x"), 1)
            run_layer(dve, cu, lo_tile, post_cu)
            run_layer(dve, cb, lo_tile, post_b)
            run_layer(dve, co, lo_tile, post_out)
            dve.wait_ge(sem("added_x"), residuals.next_total())
            vec.memset(STAT[:, 6, :], 0.0).then_inc(sem("x_ready"), 1)
        phase(act=act, pe=pe, dve=dve)

    def attention_mixer():
        rg = Region(work0)
        QK = rg("QK", [2 * N_GROUPS, DC, S])
        VV = rg("VV", [N_GROUPS, TT, D])
        stage = rg.o
        QRAW = [rg(f"QRAW{i}", [S]) for i in range(4)]
        QSQ = rg("QSQ", [S])
        QNR = [rg(f"QNR{i}", [S]) for i in range(2)]
        QST = rg("QST", [2, 4])
        rh = Region(hn0)
        QS, KS = rh("QS", [N_GROUPS, S]), rh("KS", [N_GROUPS, S])
        UB = [rh(f"UB{i}", [N_GROUPS, S]) for i in range(2)]
        assert rh.o <= work0
        rs = Region(stage)
        ES = [rs(f"ES{i}", [N_GROUPS * S]) for i in range(2)]
        rs2 = Region(rh.o)
        ETX = rs2("ETX", [N_GROUPS * S])
        assert rs2.o <= work0
        OTB = [Region(body0 + 16 * KB)("OT0", [D]), Region(body0 + 40 * KB)("OT1", [D])]
        OX = Region(work0)("OX", [DC, S])
        OXH = Region(work0 + 8 * KB)("OXH", [DC, S], f32r)
        OXL = Region(work0 + 16 * KB)("OXL", [DC, S], f32r)
        DX = Region(work0 + 24 * KB)("DXT", [DC, S])
        qk, vl, ao = (by_name[x] for x in ("qk", "v", "attn_out"))
        norm = Norm(XN, lambda c: col("norm_mix_2", DC + c))

        def pool(pool):
            pool.wait_ge(sem("hn_dead"), 1)
            with pool.Fori(0, HEADS // 2) as c:
                for x in range(2):
                    pool.wait_ge(sem("ub_free"), c * 2 + (x + 1))
                    for g in range(N_GROUPS):
                        flat = bias_rows.rearrange("g h j -> (g h j)")
                        row = flat[ds(c * (2 * 384) + (g * HEADS + x) * 384, 384)]
                        src = bass.AP(tensor=row.tensor, offset=row.offset, ap=[[1, P], [1, S]])
                        pool.dma_start(UB[x][:, g, :], src).then_inc(sem(f"ub_loaded{x}"), 16)

        def act(act):
            o = own["act"]
            norm.act(act, o)

            def ev_qk(i, u):
                n = tile_end(qk, i, u)
                act.wait_ge(mm_done, n)
                t = i * qk.U + u
                r = QRAW[u % 4]
                act_f(r[:, :], tile_bank(qk, u), ACT.Copy).then_inc(evacuated, 1)
                act.wait_ge(evacuated, n)
                act_f(QSQ[:, :], r[:, :], ACT.Square).then_inc(sem("q_sq"), 1)
                act.wait_ge(sem("q_summed"), t + 1)
                act_f(QST[:, u % 2, :], QST[:, u % 2, :], ACT.Sqrt, scale=1.0 / HD, bias=EPSC[:, 0:1]).then_inc(sem("q_root"), 1)
                act.wait_ge(sem("q_T"), t + 1)
                s = u // 8
                m = (u % 8) // 2
                dst = QK[:, ds(i * 2 + s, 1), 2 * m:2 * m + 2, (u % 2) * P:(u % 2 + 1) * P] if not isinstance(i, int) else \
                    QK[:, 2 * i + s:2 * i + s + 1, 2 * m:2 * m + 2, (u % 2) * P:(u % 2 + 1) * P]
                gcol = QKG[:, ds(i + 3 * s, 1)] if not isinstance(i, int) else QKG[:, i + 3 * s:i + 3 * s + 1]
                act_f(dst.rearrange("p a c n -> p (a c) n"), bank[4 + u % 2][:, 0:S].rearrange("p (c n) -> p c n", c=2),
                      ACT.Copy, scale=gcol).then_inc(sem("q_taken"), 1)

            def ev_v(i, u):
                act.wait_ge(mm_done, tile_end(vl, i, u))
                m = u // 2
                dst = VV[:, ds(i, 1), u % 2, m * S:(m + 1) * S].rearrange("p a n -> p (a n)") if not isinstance(i, int) \
                    else VV[:, i, u % 2, m * S:(m + 1) * S]
                act_f(dst, tile_bank(vl, u), ACT.Copy).then_inc(evacuated, 1)
            act.wait_ge(sem("gains_ready"), 2)
            run_layer(act, qk, hi_tile, ev_qk)
            run_layer(act, vl, hi_tile, ev_v)
            with act.Fori(0, HEADS // 2) as c:
                for u in range(4):
                    b = u % 2
                    n = N_GROUPS * (b + 1) * P
                    act.wait_ge(sem("b_max"), c * 4 + (u + 1))
                    act_f(ES[b][:, 0:n], PS[:, b * 1024:b * 1024 + n], ACT.Exp, bias=STAT[:, 0, b:b + 1],
                          accum_out=STAT[:, 1, b:b + 1]).then_inc(sem("b_exp"), 1)
                    if b:
                        act.wait_ge(sem("b_T"), c * 4 + (u + 1))
                        act_f(ETX[:, 512:768], bank[5][:, 0:2 * P], ACT.Copy).then_inc(sem("b_ET_act"), 1)
            for m in range(4):
                act.wait_ge(sem("x_T"), m + 1)
                act_f(OX[:, 2 * m:2 * m + 2, :], bank[m][:, :].rearrange("p (a n) -> p a n", a=2), ACT.Copy).then_inc(sem("x_full"), 1)
            act.wait_ge(sem("x_full"), 4)
            act_f(OXH[:, :, :], OX[:, :, :], ACT.Copy).then_inc(sem("ox_hi"), 1)

            def ev_out(i, u):
                act.wait_ge(mm_done, tile_end(ao, i, u))
                act_f(DX[:, i * ao.U + u, :], tile_bank(ao, u), ACT.Copy).then_inc(evacuated, 1)
            run_layer(act, ao, hi_tile, ev_out)

        def pe(pe):
            norm.pe(pe)
            norm.wait(pe)

            def transposes(i, u):
                t = i * qk.U + u
                pe.wait_ge(sem("q_normed"), t + 1)
                if not isinstance(t, int) or t >= 2:
                    pe.wait_ge(sem("q_taken"), t - 1)
                for c in range(2):
                    last = nc.tensor.transpose(bank[4 + u % 2][:, c * P:(c + 1) * P], QNR[u % 2][:, c * P:(c + 1) * P], IDENT)
                last.then_inc(sem("q_T"), 1)
            products(pe, qk, HNH, HNL, transposes)
            products(pe, vl, HNH, HNL)
            pe.wait_ge(evacuated, vl.n0 + vl.T)
            with pe.Fori(0, HEADS // 2) as c:
                def scores(u):
                    x, b = u // 2, u % 2
                    n = (b + 1) * P
                    h = slice(64 * x, 64 * x + 64)
                    if u == 0:
                        pe.wait_ge(sem("b_staged"), c + 1)
                    if b == 0:
                        pe.wait_ge(sem(f"ub_loaded{x}"), c * 48 + 48)
                    if u >= 2:
                        pe.wait_ge(sem("b_exp"), c * 4 + (u - 1))
                    for g in range(N_GROUPS):
                        o = PS[:, b * 1024 + g * n:b * 1024 + (g + 1) * n]
                        nc.tensor.matmul(o, QS[h, g, b * P:(b + 1) * P], KS[h, g, 0:n], start=True, stop=False)
                        last = nc.tensor.matmul(o, FLIP, UB[x][:, g, S - n:S], start=False, stop=True)
                    last.then_inc(sem("b_scores"), 1)

                def weigh(u):
                    x, b = u // 2, u % 2
                    nk = b + 1
                    pe.wait_ge(sem("b_exp"), c * 4 + (u + 1))
                    for j in range(N_GROUPS * nk):
                        last = nc.tensor.transpose(PS[:, 2048 + j * P:2048 + (j + 1) * P], ES[b][:, j * P:(j + 1) * P], IDENT)
                    last.then_inc(sem("b_T"), 1)
                    pe.wait_ge(sem("b_ET"), c * 4 + (u + 1))
                    if b:
                        pe.wait_ge(sem("b_ET_act"), c * 2 + (x + 1))
                    if u >= 2:
                        pe.wait_ge(sem("b_out"), c * 4 + (u - 1))
                    for j in range(N_GROUPS * nk):
                        g, kb = j // nk, j % nk
                        last = nc.tensor.matmul(bank[6 + b][:, 0:HD], ETX[:, j * P:(j + 1) * P],
                                                VV[:, g, kb, ds(c * 2 * HD + x * HD, HD)], start=j == 0,
                                                stop=j == N_GROUPS * nk - 1)
                    last.then_inc(sem("b_pv"), 1)
                scores(0)
                for u in range(4):
                    if u < 3:
                        scores(u + 1)
                    weigh(u)
            pe.wait_ge(sem("b_out"), 2 * HEADS)
            for m in range(4):
                for c in range(2):
                    for tt in range(TT):
                        last = nc.tensor.transpose(bank[m][:, c * S + tt * P:c * S + (tt + 1) * P],
                                                   OTB[tt][:, (2 * m + c) * P:(2 * m + c + 1) * P], IDENT)
                last.then_inc(sem("x_T"), 1)
            pe.wait_ge(sem("x_full"), 4)
            pe.wait_ge(sem("ox_lo"), 1)
            products(pe, ao, OXH, OXL)

        def dve(dve):
            o = own["dve"]
            norm.dve(dve, o)
            g0 = COL["attn_q_gain_2"]
            TS(QKG[:, 0:3], PRM[:, g0:g0 + 3], HD ** -0.5, None, ALU.mult).then_inc(sem("gains_ready"), 1)
            vec.tensor_copy(QKG[:, 3:6], PRM[:, g0 + 3:g0 + 6]).then_inc(sem("gains_ready"), 1)

            def post_qk(i, u):
                t = i * qk.U + u
                dve.wait_ge(sem("q_sq"), t + 1)
                st = QST[:, u % 2, :]
                vec.tensor_reduce(st, QSQ[:, :].rearrange("p (h d) -> p h d", h=4), AX.X, ALU.add).then_inc(sem("q_summed"), 1)
                dve.wait_ge(sem("q_root"), t + 1)
                vec.reciprocal(st, st).then_inc(sem("q_recip"), 1)
                dve.wait_ge(sem("q_recip"), t + 1)
                TTN(QNR[u % 2][:, :].rearrange("p (h d) -> p h d", h=4), QRAW[u % 4][:, :].rearrange("p (h d) -> p h d", h=4),
                    st.rearrange("p (h a) -> p h a", a=1).to_broadcast([P, 4, HD]), ALU.mult).then_inc(sem("q_normed"), 1)
            run_layer(dve, qk, lo_tile, post_qk)
            run_layer(dve, vl, lo_tile, lambda i, u: None)
            dve.wait_ge(evacuated, vl.n0 + vl.T)
            dve.wait_ge(sem("q_taken"), qk.T)
            vec.memset(STAT[:, 6, :], 0.0).then_inc(sem("hn_dead"), 1)
            vec.memset(STAT[:, 7, :], 0.0).then_inc(sem("ub_free"), 2)
            with o.loop(0, HEADS // 2, 1 + 4 * 1) as c:
                o.mark(vec.tensor_copy(QS[:, :, :], qk_pair(c, 0)))
                vec.tensor_copy(KS[:, :, :], qk_pair(c, 1)).then_inc(sem("b_staged"), 1)

                def peak(u):
                    b = u % 2
                    n = N_GROUPS * (b + 1) * P
                    dve.wait_ge(sem("b_scores"), c * 4 + (u + 1))
                    vec.tensor_reduce(STAT[:, 0, b:b + 1], PS[:, b * 1024:b * 1024 + n], AX.X, ALU.max,
                                      negate=True).then_inc(sem("b_max"), 1)

                def weigh(u):
                    x, b = u // 2, u % 2
                    dve.wait_ge(sem("b_T"), c * 4 + (u + 1))
                    n = 512 if b else N_GROUPS * P
                    vec.tensor_copy(ETX[:, 0:n], bank[4][:, 0:n]).then_inc(sem("b_ET"), 1)
                    o.link(vec.reciprocal(STAT[:, 4, b:b + 1], STAT[:, 1, b:b + 1]))
                    dve.wait_ge(sem("b_pv"), c * 4 + (u + 1))
                    TS(OTB[b][:, ds(c * 2 * HD + x * HD, HD)], bank[6 + b][:, 0:HD], STAT[:, 4, b:b + 1], None,
                       ALU.mult).then_inc(sem("b_out"), 1)
                    if b:
                        dve.wait_ge(sem("ub_free"), c * 2 + (2 + x))
                        vec.memset(STAT[:, 7, :], 0.0).then_inc(sem("ub_free"), 1)
                peak(0)
                for u in range(4):
                    if u < 3:
                        peak(u + 1)
                    weigh(u)
            dve.wait_ge(sem("ox_hi"), 1)
            TTN(OXL[:, :, :], OX[:, :, :], OXH[:, :, :].bitcast(f32), ALU.subtract).then_inc(sem("ox_lo"), 1)

            def post_out(i, u):
                m = i * ao.U + u
                dve.wait_ge(evacuated, tile_end(ao, i, u))
                TTN(XT[:, m, :], XT[:, m, :], DX[:, m, :], ALU.add).then_inc(sem("added_x"), 1)
            run_layer(dve, ao, lo_tile, post_out)
            dve.wait_ge(sem("added_x"), residuals.next_total())
            vec.memset(STAT[:, 6, :], 0.0).then_inc(sem("x_ready"), 1)

        def qk_pair(c, s):
            v = QK[:, :, :, :].rearrange("p (g s) c n -> p s g c n", s=2)[:, s]
            return v[:, :, ds(c, 1), :].rearrange("p g a n -> p g (a n)")
        phase(pool=pool, act=act, pe=pe, dve=dve)

    if "C" in phases:
        ffn("1_0", "norm_ffn1_2", 0)
        conv_mixer()
        ffn("2_0", "norm_ffn2_2", 0)
    if "D" in phases:
        ffn("1_1", "norm_ffn1_2", 1)
        attention_mixer()
        ffn("2_1", "norm_ffn2_2", 1)
    n_x = Norm.count if "A" in phases or "B" in phases or "C" in phases or "D" in phases else 0

    def store(sp):
        if n_x:
            sp.wait_ge(sem("x_ready"), n_x)
        else:
            sp.wait_ge(sem("x_loaded"), 16)
        sp.dma_start(out, XT[:, :, :]).then_inc(sem("stored"), 16)
        sp.wait_ge(sem("stored"), 16)
    phase(sp=store)

    with nc.Block() as block:
        @block.sync
        def _(sp):
            for part in programs["sp"]:
                part(sp)

        @block.gpsimd
        def _(pool):
            for part in programs["pool"]:
                part(pool)

        @block.scalar
        def _(act):
            own["act"] = Steps(act, sem("act_own"))
            for part in programs["act"]:
                part(act)

        @block.vector
        def _(dve):
            own["dve"] = Steps(dve, sem("dve_own"))
            for part in programs["dve"]:
                part(dve)

        @block.tensor
        def _(pe):
            for part in programs["pe"]:
                part(pe)


def columns(a):
    return np.asarray(a, np.float32).reshape(-1, P).T


def lay_out(inputs):
    a = {k: np.asarray(v) for k, v in inputs.items()}
    small, alibi, onehot = constants()
    packed = []
    for name, n in PARAMS:
        v = a[name]
        if name in ("attn_q_gain_2", "attn_k_gain_2"):
            v = np.tile(v[0], (1, 2))
        packed.append(columns(v))
        assert packed[-1].shape[1] == n, name

    def block_diagonal(w):
        o = np.zeros((2, HD, DC, 2, HD), np.float32)
        for h in range(16):
            o[h % 2, :, h // 2, h % 2, :] = w[h]
        return o.reshape(P, DC, P)

    o = {
        "params": np.concatenate(packed, axis=1),
        "small": small,
        "xT": a["x"][0].T.reshape(DC, P, S).transpose(1, 0, 2),
        "sinks": np.tile(a["attn_sinks"][0], (P, 1)),
        "bd_a": block_diagonal(a["rg_w_a"][0]),
        "bd_x": block_diagonal(a["rg_w_x"][0]),
        "alibi": alibi.reshape(P, HEADS, 2 * P),
        "router_w": a["router_w"][0].reshape(DC, P, NE).transpose(1, 0, 2),
        "router_b": np.tile(a["router_b"][0], (P, 1)),
        "expert_no": np.tile(np.arange(NE, dtype=np.float32), (P, 1)),
        "onehot": onehot,
        "rel_bias_x": np.concatenate([a["rel_bias_2"], np.full((1, N_GROUPS * HEADS), NEG, np.float32)]),
    }
    for k in ("w_ada", "w_in", "w_o_rnn", "w_o_attn", "w_out", "moe_w1", "moe_b1", "moe_w2", "moe_b2",
              "ffn1_w_in_2", "ffn1_w_out_2", "conv_w_in_2", "conv_w_out_2", "attn_w_qkv_2", "attn_w_out_2",
              "ffn2_w_in_2", "ffn2_w_out_2"):
        o[k] = a[k]
    return {k: np.ascontiguousarray(v) for k, v in o.items()}


def kernel(**inputs):
    import concourse.bacc as bacc
    from concourse.bass_utils import run_bass_kernel_spmd

    nc = bacc.Bacc("TRN2", target_bir_lowering=False, num_devices=1)
    arrays, aps = {}, {}
    for name, a in lay_out(inputs).items():
        arrays[f"in_{name}"] = a
        aps[name] = nc.dram_tensor(f"in_{name}", a.shape, mybir.dt.from_np(a.dtype), kind="ExternalInput").ap()
    out = nc.dram_tensor("out_xT", [P, DC, S], mybir.dt.float32, kind="ExternalOutput").ap()
    block_program(nc, aps, out)
    r = run_bass_kernel_spmd(nc, [arrays], core_ids=[0])
    y = np.asarray(r.results[0]["out_xT"])
    return y.transpose(1, 0, 2).reshape(D, S).T.reshape(1, S, D)
```

```python
import math
from contextlib import contextmanager

import numpy as np

import concourse.bass as bass
from concourse import mybir

P = 128
D = 1024
S = 256
DC = D // P
TT = S // P
KV = 4
HEADS = 16
HD = 64
NE = 32
TOPK = 4
FF = 1024
FF2 = 2816
FC = FF2 // P
SLOTS = 64
BUCKETS = 32
N_GROUPS = 3
EPS = 1e-6
NEG = -1e30
CONV_W = 4
CONV_W2 = 3

PARAMS = [("c", 8), ("b_ada", 48), ("norm_pre_mix", 8), ("norm_post_mix", 8), ("norm_pre_ffn", 8),
          ("norm_post_ffn", 8), ("b_in", 44), ("conv_w", 32), ("conv_b", 8), ("rg_b_a", 8),
          ("rg_b_x", 8), ("rg_lambda", 8), ("norm_ffn1_2", 16), ("norm_mix_2", 16),
          ("norm_ffn2_2", 16), ("conv_w_2", 24), ("attn_q_gain_2", 3), ("attn_k_gain_2", 3)]
COL = {}
NPAR = 0
for _name, _n in PARAMS:
    COL[_name] = NPAR
    NPAR += _n


def t5_bucket(dist):
    large = 16 + (np.log(np.maximum(dist, 1).astype(np.float32) / 16) / math.log(2048 / 16) * 16).astype(np.int32)
    return np.where(dist < 16, dist, np.minimum(large, BUCKETS - 1))


def constants():
    f = np.float32
    ident = np.eye(P, dtype=f)
    flip = ident[:, ::-1].copy()
    before = np.triu(np.ones((P, P), f), 1)
    slot = np.tile(np.arange(SLOTS, dtype=f), (P, 2))
    small = np.concatenate([ident, flip, before, slot], axis=1)
    q = np.arange(P)[:, None]
    c = np.arange(2 * P)[None, :]
    dist = q + P - c
    ok = (dist >= 0) & (dist < 128)
    slopes = np.array([2.0 ** (-8.0 * (h + 1) / HEADS) for h in range(HEADS)], f)
    alibi = np.where(ok[:, None, :], -(slopes[None, :, None] * dist[:, None, :].astype(f)), NEG).astype(f)
    d = 255 - np.arange(384)
    onehot = np.zeros((BUCKETS + 1, N_GROUPS, 384), f)
    for g, (window, dil) in enumerate(((128, 1), (512, 4), (2048, 16))):
        seen = (d >= 0) & (d % dil == 0) & (d <= window)
        b = t5_bucket(np.clip(d, 0, window))
        for j in range(384):
            onehot[b[j] if seen[j] else BUCKETS, g, j] = 1.0
    return small, alibi.reshape(P, HEADS * 2 * P), onehot.reshape(BUCKETS + 1, N_GROUPS * 384)


class Steps:

    def __init__(self, eng, sem):
        self.eng, self.sem, self.n = eng, sem, 0
        self.k = 0

    def mark(self, ins):
        ins.then_inc(self.sem, 1)
        self.n = self.n + 1
        self.k += 1

    def wait(self):
        self.eng.wait_ge(self.sem, self.n)

    def link(self, ins):
        self.mark(ins)
        self.wait()

    @contextmanager
    def loop(self, start, end, per):
        base, k = self.n, self.k
        with self.eng.Fori(start, end) as i:
            self.n = base + (i - start) * per
            yield i
        assert self.k - k == per, (self.k - k, per)
        self.n = base + (end - start) * per


class Layer:

    def __init__(self, name, tiles, kc, src, tok=False, load_turn=None):
        self.name, self.T, self.kc, self.src, self.tok = name, tiles, kc, src, tok
        self.tpg = 2 if kc == DC else 1
        self.slots = 4 if kc == DC else 2
        self.U = 4 * self.tpg
        self.G = tiles // self.tpg
        self.gu = self.U // self.tpg
        self.lgu = (load_turn or self.U) // self.tpg


def units(eng, lo, hi, unroll, body):
    t = lo
    while t < hi:
        whole = (hi - t) // unroll
        if t % unroll == 0 and whole >= 2:
            with eng.Fori(t // unroll, t // unroll + whole) as i:
                for u in range(unroll):
                    body(i, u)
            t += whole * unroll
        else:
            body(t // unroll, t % unroll)
            t += 1


def block_program(nc, A, out, phases="ABCD"):
    f32, f32r, i32, u32 = mybir.dt.float32, mybir.dt.float32r, mybir.dt.int32, mybir.dt.uint32
    ALU, ACT, AX = mybir.AluOpType, mybir.ActivationFunctionType, mybir.AxisListType
    ds = bass.ds

    top = nc.sbuf_usable_end
    KB = 1024

    class Region:

        def __init__(self, offset):
            self.o = offset

        def __call__(self, name, free, dt=f32):
            n = (int(np.prod(free)) * 4 + 31) // 32 * 32
            assert self.o + n <= top, (name, self.o + n, top)
            t = nc.alloc_sbuf_tensor_at(name, [P] + list(free), dt, offset=self.o)
            self.o += n
            return t

    r0 = Region((nc.sbuf_base + 63) // 64 * 64)
    PRM = r0("PRM", [NPAR])
    SM = r0("SM", [4 * P])
    IDENT, FLIP, BEFORE, SLOT = (SM[:, i * P:(i + 1) * P] for i in range(4))
    MEAN = r0("MEAN", [P])
    ONE = r0("ONE", [P])
    EPSC = r0("EPSC", [1])
    XT = r0("XT", [DC, S])
    ADA = r0("ADA", [48])
    ADV = r0("ADV", [4, DC])
    RS = r0("RS", [S])
    SD = r0("SD", [S])
    LAMV = r0("LAMV", [6, DC])
    SINK = r0("SINK", [2, HEADS])
    CSIL = r0("CSIL", [DC])
    STAT = r0("STAT", [8, 2])
    QKG = r0("QKG", [6])
    raw0 = r0.o
    RAW = [r0(f"RAW{s}", [FC * P]) for s in range(4)]
    body0 = r0.o
    WHI = r0("WHI", [48 * P], f32r)
    WLO = r0("WLO", [48 * P], f32r)
    hn0 = r0.o
    HNH = r0("HNH", [DC, S], f32r)
    HNL = r0("HNL", [DC, S], f32r)
    work0 = r0.o

    PS = nc.alloc_psum_tensor("PS", [P, 8 * 512], f32)
    bank = [PS[:, b * 512:(b + 1) * 512] for b in range(8)]
    bias_rows = nc.dram_tensor("bias_rows", [N_GROUPS, HEADS, 384], f32, kind="Internal").ap()

    made = {}

    def sem(name):
        if name not in made:
            made[name] = nc.alloc_semaphore(name)
        return made[name]

    raw_loaded = [sem(f"raw_loaded{s}") for s in range(4)]
    hi_done, lo_done = sem("hi_done"), sem("lo_done")
    mm_done, evacuated = sem("mm_done"), sem("evacuated")

    def cols(w, c0=0, width=256, step=0):
        v = w.rearrange("(k p) n -> p k n", p=P)

        def src(i, gu, per_turn):
            move = step or width * per_turn
            if isinstance(i, int):
                return v[:, :, i * move + c0 + width * gu:i * move + c0 + width * (gu + 1)]
            return v[:, :, ds(i * move + (c0 + width * gu), width)]
        return src

    layers = []
    if "A" in phases:
        layers += [Layer("win", 44, DC, cols(A["w_in"][0])),
                   Layer("wor", 8, DC, cols(A["w_o_rnn"][0])),
                   Layer("woa", 8, DC, cols(A["w_o_attn"][0])),
                   Layer("wout", 8, DC, cols(A["w_out"][0]))]

    def ffn_layers(tag, w_in, w_out):
        return [Layer(f"gate{tag}", FC, DC, cols(w_in)),
                Layer(f"up{tag}", FC, DC, cols(w_in, FF2)),
                Layer(f"down{tag}", DC, FC, cols(w_out, 0, P))]

    if "C" in phases:
        layers += ffn_layers("1_0", A["ffn1_w_in_2"][0], A["ffn1_w_out_2"][0])
        layers += [Layer("conv_cu", 16, DC, cols(A["conv_w_in_2"][0], D)),
                   Layer("conv_b", 8, DC, cols(A["conv_w_in_2"][0], 0)),
                   Layer("conv_out", 8, DC, cols(A["conv_w_out_2"][0]))]
        layers += ffn_layers("2_0", A["ffn2_w_in_2"][0], A["ffn2_w_out_2"][0])
    if "D" in phases:
        layers += ffn_layers("1_1", A["ffn1_w_in_2"][1], A["ffn1_w_out_2"][1])
        qkv = A["attn_w_qkv_2"][0]
        layers += [Layer("qk", 48, DC, cols(qkv, 0, 256, 3 * D), tok=True, load_turn=16),
                   Layer("v", 24, DC, cols(qkv, 2 * D, 256, 3 * D), tok=True),
                   Layer("attn_out", 8, DC, cols(A["attn_w_out_2"][0]))]
        layers += ffn_layers("2_1", A["ffn2_w_in_2"][1], A["ffn2_w_out_2"][1])
    fresh = {layers[0].name} if layers else set()
    if "B" in phases and "C" in phases:
        fresh.add("gate1_0")
    group_end = []
    n = g = 0
    for idx, L in enumerate(layers):
        L.n0, L.g0, L.idx = n, g, idx
        group_end += [n + (j + 1) * L.tpg for j in range(L.G)]
        n, g = n + L.T, g + L.G
    by_name = {L.name: L for L in layers}

    def load_layer(sp, L):
        def one(i, gu):
            s = (L.g0 + gu) % 4
            dst = RAW[s][:, 0:L.kc * L.tpg * P].rearrange("p (k n) -> p k n", k=L.kc)
            if not isinstance(i, int):
                sp.wait_ge(lo_done, i * L.lgu * L.tpg + (L.n0 + (gu - 3) * L.tpg))
            elif L.g0 + i * L.lgu + gu >= 4:
                sp.wait_ge(lo_done, group_end[L.g0 + i * L.lgu + gu - 4])
            sp.dma_start(dst, L.src(i, gu, L.lgu)).then_inc(raw_loaded[s], 16)
        for gu in range(min(L.lgu, L.G)):
            one(0, gu)
        units(sp, min(L.lgu, L.G), L.G, L.lgu, one)

    def raw_tile(L, i, u):
        G = L.g0 + u // L.tpg
        v = RAW[G % 4][:, 0:L.kc * L.tpg * P].rearrange("p (k n) -> p k n", k=L.kc)
        h = u % L.tpg
        return G % 4, v[:, :, h * P:(h + 1) * P], i * (4 * L.gu) + 16 * (G // 4 + 1)

    def split_tile(W, L, u):
        o = (L.n0 + u) % L.slots * (DC if L.kc == DC else 24)
        return W[:, o * P:(o + L.kc) * P].rearrange("p (k n) -> p k n", k=L.kc)

    def hi_tile(act, L, i, u):
        n = i * L.U + (L.n0 + u)
        s, raw, landed = raw_tile(L, i, u)
        act.wait_ge(raw_loaded[s], landed)
        first = isinstance(i, int) and i * L.U + u < L.slots
        prev = layers[L.idx - 1] if first and L.idx else None
        if prev is not None and prev.slots != L.slots:
            act.wait_ge(mm_done, L.n0)
        else:
            paired = L.tok or (prev is not None and prev.tok)
            back = L.slots - 1 - (1 if paired and (L.n0 + u) % 2 == 0 else 0)
            if not isinstance(n, int) or n > back:
                act.wait_ge(mm_done, n - back)
        nc.scalar.activation(split_tile(WHI, L, u), raw, ACT.Copy).then_inc(hi_done, 1)

    def lo_tile(dve, L, i, u):
        _, raw, _ = raw_tile(L, i, u)
        dve.wait_ge(hi_done, i * L.U + (L.n0 + u + 1))
        nc.vector.tensor_tensor(split_tile(WLO, L, u), raw, split_tile(WHI, L, u).bitcast(f32),
                                ALU.subtract).then_inc(lo_done, 1)

    def back(L, i, u, k):
        return i + (u - k) // L.U, (u - k) % L.U

    def run_layer(eng, L, make, work, peel=0):
        nxt = layers[L.idx + 1] if L.idx + 1 < len(layers) else None
        if nxt is not None and nxt.name in fresh:
            nxt = None
        if L.name in fresh:
            for u in range(L.slots):
                make(eng, L, 0, u)

        def both(i, u):
            work(i, u)
            make(eng, L, i + (u + L.slots) // L.U, (u + L.slots) % L.U)
        for t in range(peel):
            both(t // L.U, t % L.U)
        units(eng, peel, L.T - L.slots, L.U, both)
        for m in range(L.T - L.slots, L.T):
            work(m // L.U, m % L.U)
            if nxt is not None and nxt.slots == L.slots:
                make(eng, nxt, 0, m + L.slots - L.T)
        if nxt is not None and nxt.slots != L.slots:
            for u in range(nxt.slots):
                make(eng, nxt, 0, u)

    def products(pe, L, xh, xl, behind=None, feed=None):
        def one(i, u):
            n = i * L.U + (L.n0 + u)
            if not L.tok or u % 2 == 0:
                pe.wait_ge(lo_done, n + (2 if L.tok else 1))
            if not isinstance(n, int) or n >= 4:
                pe.wait_ge(evacuated, n - 3)
            if not L.tok:
                hi, lo = split_tile(WHI, L, u), split_tile(WLO, L, u)
                terms = [(w[:, k, :], x[:, k, :]) for k in range(L.kc)
                         for w, x in ((hi, xh), (hi, xl), (lo, xh))]
            else:
                tt, s = u % 2, (L.n0 + u) % 4 - u % 2
                wh, wl = (W[:, 0:32 * P].rearrange("p (s k n) -> p s k n", s=4, k=DC)[:, s:s + 2] for W in (WHI, WLO))
                terms = [(x[:, k, tt * P:(tt + 1) * P], w[:, :, k, :]) for k in range(DC)
                         for x, w in ((xh, wh), (xh, wl), (xl, wh))]
            o = bank[(L.n0 + u) % 4][:, 0:S]
            if L.tok:
                o = o.rearrange("p (a n) -> p a n", a=2)
            for j, (a, r) in enumerate(terms):
                if feed is not None and u == 0 and j % 3 == 0:
                    feed(pe, j // 3)
                last = nc.tensor.matmul(o, a, r, start=j == 0, stop=j == len(terms) - 1)
            last.then_inc(mm_done, 1)
            if behind is not None and (not isinstance(i, int) or i * L.U + u >= 2):
                behind(i + (u - 2) // L.U, (u - 2) % L.U)
        for u in range(min(4, L.T) if L.n0 == 0 else 0):
            one(0, u)
        start = 4 if L.n0 == 0 else 2 if behind is not None else 0
        for u in range(0 if L.n0 == 0 else start):
            one(0, u)
        units(pe, start, L.T, L.U, one)
        if behind is not None:
            for t in (L.T - 2, L.T - 1):
                behind(t // L.U, t % L.U)

    def tile_bank(L, u):
        return bank[(L.n0 + u) % 4][:, 0:S]

    def tile_end(L, i, u):
        return i * L.U + (L.n0 + u + 1)

    def chunk(t, j):
        if isinstance(j, int):
            return t[:, j, :]
        return t[:, ds(j, 1), :].rearrange("p a s -> p (a s)")

    def col(name, j=0):
        o = COL[name]
        if isinstance(j, int):
            return PRM[:, o + j:o + j + 1]
        return PRM[:, ds(j + o, 1)]

    act_f, vec = nc.scalar.activation, nc.vector
    TS, TTN, STT = vec.tensor_scalar, vec.tensor_tensor, vec.scalar_tensor_tensor

    updates = {"whole": 0, "chunks": 0}

    class Norm:
        count = 0
        splits = 0

        def __init__(self, T, gain, shift=None, keep=False, early=False):
            self.k, self.T, self.gain, self.shift, self.keep, self.early = Norm.count, T, gain, shift, keep, early
            self.h, self.whole = Norm.splits, updates["whole"]
            Norm.count += 1
            Norm.splits += 0 if keep else 1

        def square(self, act, c):
            act_f(self.T[:, c, :], XT[:, c, :], ACT.Square).then_inc(sem("squared"), 1)

        def add_mean(self, pe, c):
            pe.wait_ge(sem("squared"), DC * self.k + c + 1)
            ins = nc.tensor.matmul(bank[6][:, 0:S], MEAN[:, :], self.T[:, c, :], start=c == 0, stop=c == DC - 1)
            if c == DC - 1:
                ins.then_inc(sem("mean_done"), 1)

        def act(self, act, own):
            k, T = self.k, self.T
            if not self.early:
                if k:
                    act.wait_ge(sem("x_ready"), self.whole)
                else:
                    act.wait_ge(sem("x_loaded"), 16)
                for c in range(DC):
                    self.square(act, c)
            act.wait_ge(sem("mean_done"), k + 1)
            act_f(SD[:, :], bank[6][:, 0:S], ACT.Sqrt, bias=EPSC[:, 0:1]).then_inc(sem("root_done"), 1)
            for c in range(DC):
                act.wait_ge(sem("scaled"), DC * k + c + 1)
                bias = self.shift(c) if self.shift else 0.0
                if self.keep:
                    act_f(T[:, c, :], T[:, c, :], ACT.Identity, bias=bias).then_inc(sem("kept"), 1)
                else:
                    act_f(HNH[:, c, :], T[:, c, :], ACT.Identity, bias=bias).then_inc(sem("hn_hi"), 1)

        def pe(self, pe):
            if not self.early:
                for c in range(DC):
                    self.add_mean(pe, c)

        def dve(self, dve, own):
            k, T = self.k, self.T

            def low(c):
                dve.wait_ge(sem("hn_hi"), DC * self.h + c + 1)
                if self.shift:
                    ins = STT(HNL[:, c, :], T[:, c, :], self.shift(c), HNH[:, c, :].bitcast(f32), ALU.add, ALU.subtract)
                else:
                    ins = TTN(HNL[:, c, :], T[:, c, :], HNH[:, c, :].bitcast(f32), ALU.subtract)
                ins.then_inc(sem("hn_lo"), 1)
            dve.wait_ge(sem("root_done"), k + 1)
            own.link(vec.reciprocal(RS[:, :], SD[:, :]))
            for c in range(DC):
                STT(T[:, c, :], XT[:, c, :], self.gain(c), RS[:, :], ALU.mult, ALU.mult).then_inc(sem("scaled"), 1)
                if c and not self.keep:
                    low(c - 1)
            if not self.keep:
                low(DC - 1)

        def feed(self, pe, k):
            pe.wait_ge(sem("hn_lo"), DC * self.h + k + 1)

    programs = {"sp": [], "pool": [], "act": [], "dve": [], "pe": []}
    own = {}

    def phase(**parts):
        for name, f in parts.items():
            programs[name].append(f)
    ra = Region(work0)
    AW = [ra(f"AW{s}", [DC, D]) for s in range(2)]
    AROW = ra("AROW", [6, S])

    def setup_sp(sp):
        sp.dma_start(PRM[:, :], A["params"]).then_inc(sem("prm_loaded"), 16)
        sp.dma_start(SM[:, :], A["small"]).then_inc(sem("small_loaded"), 16)
        sp.dma_start(XT[:, :, :], A["xT"]).then_inc(sem("x_loaded"), 16)
        sp.dma_start(SINK[:, 0, :], A["sinks"]).then_inc(sem("sinks_loaded"), 16)
        aw = A["w_ada"][0].rearrange("(k p) n -> p k n", p=P)
        for r in range(6):
            if r >= 2:
                sp.wait_ge(sem("ada_mm"), r - 1)
            sp.dma_start(AW[r % 2][:, :, :], aw[:, :, D * r:D * (r + 1)]).then_inc(sem(f"aw_loaded{r % 2}"), 16)

    def setup_pool(pool):
        nc.gpsimd.memset(MEAN[:, :], 1.0 / D).then_inc(sem("filled"), 1)
        nc.gpsimd.memset(ONE[:, :], 1.0).then_inc(sem("filled"), 1)
        nc.gpsimd.memset(EPSC[:, :], EPS).then_inc(sem("filled"), 1)
        nc.gpsimd.memset(AROW[:, :, :], 0.0).then_inc(sem("filled"), 1)

    def setup_act(act):
        act.wait_ge(sem("filled"), 4)
        act.wait_ge(sem("prm_loaded"), 16)
        act_f(CSIL[:, :], PRM[:, COL["c"]:COL["c"] + DC], ACT.Silu).then_inc(sem("silu_c"), 1)
        for r in range(6):
            act.wait_ge(sem("ada_mm"), r + 1)
            for g in range(4):
                row = slice(32 * g, 32 * g + 1)
                act_f(AROW[row, r, :], bank[r][row, 0:S], ACT.Copy).then_inc(sem("ada_row"), 1)
        act.wait_ge(sem("ada_ready"), 5)

    def setup_pe(pe):
        pe.wait_ge(sem("filled"), 4)
        pe.wait_ge(sem("small_loaded"), 16)
        pe.wait_ge(sem("silu_c"), 1)
        def columns(r):
            pe.wait_ge(sem("ada_row"), 4 * r + 4)
            for c in range(DC):
                g = 32 * (c // 2)
                last = nc.tensor.matmul(bank[7][:, DC * r + c:DC * r + c + 1], AROW[:, r, (c % 2) * P:(c % 2 + 1) * P],
                                        IDENT[:, g:g + 1], start=True, stop=True)
            last.then_inc(sem("ada_col"), 1)
        for r in range(6):
            pe.wait_ge(sem(f"aw_loaded{r % 2}"), 16 * (r // 2 + 1))
            for k in range(DC):
                for g in range(4):
                    last = nc.tensor.matmul(bank[r][32 * g:32 * g + 1, 0:S], CSIL[:, k:k + 1],
                                            AW[r % 2][:, k, S * g:S * (g + 1)], start=k == 0, stop=k == DC - 1,
                                            tile_position=(0, 32 * g))
            last.then_inc(sem("ada_mm"), 1)
            if r >= 1:
                columns(r - 1)
        columns(5)

    def setup_dve(dve):
        dve.wait_ge(sem("prm_loaded"), 16)
        dve.wait_ge(sem("ada_col"), 6)
        TTN(ADA[:, :], bank[7][:, 0:48], PRM[:, COL["b_ada"]:COL["b_ada"] + 48], ALU.add).then_inc(sem("ada_ready"), 1)
        dve.wait_ge(sem("ada_ready"), 1)
        for r, (part, gain, plus) in enumerate(((1, "norm_pre_mix", 1.0), (2, "norm_post_mix", 0.0),
                                                (4, "norm_pre_ffn", 1.0), (5, "norm_post_ffn", 0.0))):
            STT(ADV[:, r, :], ADA[:, part * DC:(part + 1) * DC], plus,
                PRM[:, COL[gain]:COL[gain] + DC], ALU.add, ALU.mult).then_inc(sem("ada_ready"), 1)
        dve.wait_ge(sem("ada_ready"), 5)

    phase(sp=setup_sp, pool=setup_pool, act=setup_act, pe=setup_pe, dve=setup_dve)
    for L in layers:
        if L.name == "gate1_0" and "B" in phases:
            phase(sp=lambda sp: expert_loads(sp))
        phase(sp=lambda sp, L=L: load_layer(sp, L))
    if "B" in phases and "C" not in phases:
        phase(sp=lambda sp: expert_loads(sp))

    def bias_tables():
        rt = Region(work0)
        RB = rt("RB", [N_GROUPS * HEADS])
        OH = rt("OHB", [N_GROUPS, 384])
        RT = rt("RT", [N_GROUPS, 384])

        def pool(pool):
            pool.wait_ge(sem("ada_ready"), 5)
            pool.dma_start(RB[0:BUCKETS + 1, :], A["rel_bias_x"]).then_inc(sem("rb_loaded"), 16)
            pool.dma_start(OH[0:BUCKETS + 1, :, :], A["onehot"].rearrange("b (g j) -> b g j", g=N_GROUPS)).then_inc(sem("rb_loaded"), 16)
            pool.wait_ge(sem("rows_ready"), N_GROUPS)
            pool.dma_start(bias_rows.rearrange("g h j -> h g j"), RT[0:HEADS, :, :]).then_inc(sem("rows_stored"), 16)
            pool.wait_ge(sem("rows_stored"), 16)

        def pe(pe):
            pe.wait_ge(sem("rb_loaded"), 32)
            for g in range(N_GROUPS):
                nc.tensor.matmul(bank[g][0:HEADS, 0:384], RB[0:BUCKETS + 1, g * HEADS:(g + 1) * HEADS],
                                 OH[0:BUCKETS + 1, g, :], start=True, stop=True).then_inc(sem("rows_mm"), 1)

        def act(act):
            for g in range(N_GROUPS):
                act.wait_ge(sem("rows_mm"), g + 1)
                act_f(RT[0:HEADS, g, :], bank[g][0:HEADS, 0:384], ACT.Copy).then_inc(sem("rows_ready"), 1)
            act.wait_ge(sem("rows_stored"), 16)

        phase(pool=pool, pe=pe, act=act)

    if "D" in phases:
        bias_tables()

    def mixer():
        ra = Region(work0)
        PROJ = ra("PROJ", [44, S])
        XC = ra("XC", [DC, S])
        T1 = ra("T1", [DC, S])
        T2 = ra("T2", [DC, S])
        ya = ra.o
        YAH = ra("YAH", [DC, S], f32r)
        YAL = ra("YAL", [DC, S], f32r)
        rb = Region(ya)
        BDA, BDX = rb("BDA", [DC, P]), rb("BDX", [DC, P])
        T3 = rb("T3", [DC, S])
        rh = Region(hn0)
        YRH, YRL = rh("YRH", [DC, S], f32r), rh("YRL", [DC, S], f32r)
        rh = Region(hn0)
        MGH, MGL = rh("MGH", [DC, S], f32r), rh("MGL", [DC, S], f32r)
        ALB = Region(work0)("ALB", [HEADS, S])
        OF = Region(work0)("OF", [DC, S])
        rx = Region(work0 + 44 * KB)
        KD = rx("KD", [KV, S])
        VT = rx("VT", [TT, KV * HD])
        QS = rx("QS", [2, S])
        KS = rx("KS", [S])
        ES = [rx(f"AES{i}", [S]) for i in range(2)]
        ET = [rx(f"AET{i}", [S]) for i in range(2)]
        OT = rx("AOT", [TT, D])
        assert rx.o <= ya
        XR, GR, Q, K_, V_ = PROJ[:, 0:8, :], PROJ[:, 8:16, :], 16, 24, 26
        win, wor, woa, wout = (by_name[x] for x in ("win", "wor", "woa", "wout"))
        norm = Norm(T1, lambda c: ADV[:, 0, c:c + 1], lambda c: ADA[:, c:c + 1])

        def pool(pool):
            pool.wait_ge(sem("ada_ready"), 1)
            pool.dma_start(BDA[:, :, :], A["bd_a"]).then_inc(sem("bd_loaded"), 16)
            pool.dma_start(BDX[:, :, :], A["bd_x"]).then_inc(sem("bd_loaded"), 16)
            pool.wait_ge(sem("yr_lo"), 1)
            pool.dma_start(ALB[:, :, :], A["alibi"]).then_inc(sem("alibi_loaded"), 16)
            for j in range(KV):
                k = PROJ[64 * (j % 2):64 * (j % 2) + 64, K_ + j // 2, :]
                pool.dma_start(KD[0:64, j, :], k).then_inc(sem("kd_loaded"), 16)
                pool.dma_start(KD[64:128, j, :], k).then_inc(sem("kd_loaded"), 16)

        def evac_into(act, L, dst):
            def ev(i, u):
                act.wait_ge(mm_done, tile_end(L, i, u))
                act_f(chunk(dst, i * L.U + u), tile_bank(L, u), ACT.Copy).then_inc(evacuated, 1)
            return ev

        def act(act):
            o = own["act"]
            norm.act(act, o)
            act.wait_ge(sem("lam_abs"), 1)
            act_f(LAMV[:, 1, :], LAMV[:, 1, :], ACT.Exp, scale=-1.0).then_inc(sem("lam_exp"), 1)

            def ev_win(i, u):
                act.wait_ge(mm_done, tile_end(win, i, u))
                m = i * win.U + u
                act_f(chunk(PROJ, m), tile_bank(win, u), ACT.Identity, bias=col("b_in", m)).then_inc(evacuated, 1)
            run_layer(act, win, hi_tile, ev_win)
            for c in range(DC):
                act.wait_ge(sem("gates_mm"), c + 1)
                b = bank[4 + c % 2]
                o.mark(act_f(T1[:, c, :], b[:, 0:S], ACT.Sigmoid, bias=col("rg_b_a", c)))
                act_f(T2[:, c, :], b[:, S:2 * S], ACT.Sigmoid, bias=col("rg_b_x", c)).then_inc(sem("gates_out"), 1)
            o.wait()
            act.wait_ge(sem("lam_ready"), 1)
            for c in range(DC):
                act_f(T1[:, c, :], T1[:, c, :], ACT.Tanh, scale=LAMV[:, 4, c:c + 1]).then_inc(sem("half_tanh"), 1)
            act.wait_ge(sem("tanh_read"), 1)
            act_f(T1[:, :, :], T1[:, :, :], ACT.Sqrt).then_inc(sem("lru_root"), 1)
            act.wait_ge(sem("lru_in"), 1)
            act_f(T1[:, :, :], GR, ACT.Square).then_inc(sem("gelu_sq"), 1)
            act.wait_ge(sem("gelu_in"), 1)
            act_f(T1[:, :, :], T1[:, :, :], ACT.Tanh, scale=math.sqrt(2.0 / math.pi)).then_inc(sem("gelu_tanh"), 1)
            act.wait_ge(sem("y_rnn"), 1)
            act_f(YRH[:, :, :], T1[:, :, :], ACT.Copy).then_inc(sem("yr_hi"), 1)
            act.wait_ge(sem("v_T"), 1)
            act_f(VT[:, :, :], bank[4][:, :].rearrange("p (t n) -> p t n", t=TT), ACT.Copy).then_inc(sem("v_ready"), 1)
            with act.Fori(0, KV) as j:
                for u in range(8):
                    b = u % 2
                    n = (b + 1) * P
                    act.wait_ge(sem("a_max"), j * 8 + (u + 1))
                    act_f(ES[b][:, 0:n], bank[b][:, 0:n], ACT.Exp, bias=STAT[:, 0, b:b + 1],
                          accum_out=STAT[:, 1, b:b + 1]).then_inc(sem("a_exp"), 1)
                    act_f(STAT[:, 2, b:b + 1], SINK[:, 0, ds(j * 4 + u // 2, 1)], ACT.Exp,
                          bias=STAT[:, 0, b:b + 1]).then_inc(sem("a_sink"), 1)
            for m in range(4):
                act.wait_ge(sem("o_T"), m + 1)
                act_f(OF[:, 2 * m:2 * m + 2, :], bank[m][:, :].rearrange("p (a n) -> p a n", a=2),
                      ACT.Copy).then_inc(sem("o_full"), 1)
            act.wait_ge(sem("o_full"), 4)
            act_f(YAH[:, :, :], OF[:, :, :], ACT.Copy).then_inc(sem("ya_hi"), 1)
            act_f(PROJ[:, 28:44, :], PROJ[:, 28:44, :], ACT.Sigmoid).then_inc(sem("merge_gates"), 1)
            run_layer(act, wor, hi_tile, evac_into(act, wor, T2))
            run_layer(act, woa, hi_tile, evac_into(act, woa, T1))
            run_layer(act, wout, hi_tile, evac_into(act, wout, T1))
            act.wait_ge(evacuated, wout.n0 + 8)
            act_f(T2[:, :, :], T1[:, :, :], ACT.Square).then_inc(sem("post_sq"), 1)
            act.wait_ge(sem("post_mean"), 1)
            act_f(SD[:, :], bank[6][:, 0:S], ACT.Sqrt, bias=EPSC[:, 0:1]).then_inc(sem("post_root"), 1)

        def pe(pe):
            norm.pe(pe)
            products(pe, win, HNH, HNL, feed=norm.feed)
            pe.wait_ge(sem("bd_loaded"), 32)
            for c in range(DC):
                pe.wait_ge(sem("conv_done"), c + 1)
                if c >= 2:
                    pe.wait_ge(sem("gates_out"), c - 1)
                b = bank[4 + c % 2]
                nc.tensor.matmul(b[:, 0:S], BDA[:, c, :], XC[:, c, :], start=True, stop=True)
                nc.tensor.matmul(b[:, S:2 * S], BDX[:, c, :], XC[:, c, :], start=True, stop=True)\
                    .then_inc(sem("gates_mm"), 1)
            pe.wait_ge(sem("lru_in"), 1)
            for tt in range(TT):
                for m in range(2):
                    last = nc.tensor.transpose(bank[4][:, (2 * tt + m) * P:(2 * tt + m + 1) * P],
                                               PROJ[:, V_ + m, tt * P:(tt + 1) * P], IDENT)
            last.then_inc(sem("v_T"), 1)
            pe.wait_ge(sem("v_ready"), 1)
            pe.wait_ge(sem("alibi_loaded"), 16)
            with pe.Fori(0, KV) as j:
                def scores(u):
                    x, b = u // 2, u % 2
                    n = (b + 1) * P
                    h = slice(64 * (x % 2), 64 * (x % 2) + 64)
                    if u == 0:
                        pe.wait_ge(sem("a_staged"), j + 1)
                    if u >= 2:
                        pe.wait_ge(sem("a_exp"), j * 8 + (u - 1))
                    nc.tensor.matmul(bank[b][:, 0:n], QS[h, x // 2, b * P:(b + 1) * P], KS[h, 0:n], start=True, stop=False)
                    nc.tensor.matmul(bank[b][:, 0:n], IDENT, chunk(ALB, j * 4 + x)[:, S - n:S], start=False, stop=True)\
                        .then_inc(sem("a_scores"), 1)

                def weigh(u):
                    x, b = u // 2, u % 2
                    pe.wait_ge(sem("a_exp"), j * 8 + (u + 1))
                    for kb in range(b + 1):
                        last = nc.tensor.transpose(bank[2 + b][:, kb * P:(kb + 1) * P], ES[b][:, kb * P:(kb + 1) * P], IDENT)
                    last.then_inc(sem("a_T"), 1)
                    pe.wait_ge(sem("a_ET"), j * 8 + (u + 1))
                    if u >= 2:
                        pe.wait_ge(sem("a_out"), j * 8 + (u - 1))
                    for kb in range(b + 1):
                        last = nc.tensor.matmul(bank[4 + b][:, 0:HD], ET[b][:, kb * P:(kb + 1) * P],
                                                VT[:, kb, ds(j * HD, HD)], start=kb == 0, stop=kb == b)
                    last.then_inc(sem("a_pv"), 1)
                scores(0)
                for u in range(8):
                    if u < 7:
                        scores(u + 1)
                    weigh(u)
            pe.wait_ge(sem("a_out"), 8 * KV)
            for m in range(4):
                for c in range(2):
                    for tt in range(TT):
                        last = nc.tensor.transpose(bank[m][:, c * S + tt * P:c * S + (tt + 1) * P],
                                                   OT[:, tt, (2 * m + c) * P:(2 * m + c + 1) * P], IDENT)
                last.then_inc(sem("o_T"), 1)
            pe.wait_ge(sem("o_full"), 4)
            pe.wait_ge(sem("yr_lo"), 1)
            products(pe, wor, YRH, YRL)
            pe.wait_ge(sem("ya_lo"), 1)
            products(pe, woa, YAH, YAL)
            pe.wait_ge(sem("merged"), 8)
            products(pe, wout, MGH, MGL)
            pe.wait_ge(sem("post_sq"), 1)
            for c in range(DC):
                last = nc.tensor.matmul(bank[6][:, 0:S], MEAN[:, :], T2[:, c, :], start=c == 0, stop=c == DC - 1)
            last.then_inc(sem("post_mean"), 1)

        def dve(dve):
            o = own["dve"]
            norm.dve(dve, o)
            lam = PRM[:, COL["rg_lambda"]:COL["rg_lambda"] + DC]
            neg, e, z, z2, pz, den = (LAMV[:, r, :] for r in range(6))
            o.link(TS(neg, lam, -1.0, None, ALU.mult))
            TTN(e, neg, lam, ALU.max).then_inc(sem("lam_abs"), 1)
            dve.wait_ge(sem("lam_exp"), 1)
            o.link(TS(den, e, 2.0, None, ALU.add))
            o.link(vec.reciprocal(z2, den))
            o.link(TTN(z, e, z2, ALU.mult))
            o.link(TTN(z2, z, z, ALU.mult))
            o.link(vec.memset(pz, 1.0 / 17))
            for k in (15, 13, 11, 9, 7, 5, 3, 1):
                o.link(TTN(pz, pz, z2, ALU.mult))
                o.link(TS(pz, pz, 1.0 / k, None, ALU.add))
            o.link(STT(pz, pz, 2.0, z, ALU.mult, ALU.mult))
            o.link(TS(neg, neg, 0.0, None, ALU.max))
            o.link(TTN(pz, pz, neg, ALU.add))
            TS(pz, pz, 4.0, None, ALU.mult).then_inc(sem("lam_ready"), 1)
            dve.wait_ge(sem("sinks_loaded"), 16)
            o.link(TS(SINK[:, 1, :], SINK[:, 0, :], -1.0, None, ALU.mult))
            run_layer(dve, win, lo_tile, lambda i, u: None)
            dve.wait_ge(evacuated, win.n0 + 44)
            for c in range(DC):
                x, y = PROJ[:, c, :], XC[:, c, :]
                o.link(TS(y, x, col("conv_w", 3 * DC + c), col("conv_b", c), ALU.mult, ALU.add))
                for lag in (1, 2):
                    o.link(STT(y[:, lag:S], x[:, 0:S - lag], col("conv_w", (3 - lag) * DC + c), y[:, lag:S], ALU.mult, ALU.add))
                STT(y[:, 3:S], x[:, 0:S - 3], col("conv_w", c), y[:, 3:S], ALU.mult, ALU.add).then_inc(sem("conv_done"), 1)
            dve.wait_ge(sem("half_tanh"), DC)
            o.link(TS(T3[:, :, :], T1[:, :, :], 1.0, None, ALU.add))
            o.link(vec.reciprocal(XR, T3[:, :, :]))
            o.link(TTN(T3[:, :, :], T1[:, :, :], XR, ALU.mult))
            TTN(T3[:, :, :], XR, T3[:, :, :], ALU.subtract).then_inc(sem("tanh_read"), 1)
            o.link(TTN(T2[:, :, :], T2[:, :, :], XC[:, :, :], ALU.mult))
            dve.wait_ge(sem("lru_root"), 1)
            o.link(STT(T1[:, :, :], T1[:, :, :], 2.0, XR, ALU.mult, ALU.mult))
            o.link(vec.memset(T1[:, :, 0:1], 1.0))
            TTN(T2[:, :, :], T2[:, :, :], T1[:, :, :], ALU.mult).then_inc(sem("lru_in"), 1)
            dve.wait_ge(sem("lru_in"), 1)
            for c in range(DC):
                o.mark(vec.tensor_tensor_scan(XC[:, c, :], T3[:, c, :], T2[:, c, :], 0.0, ALU.mult, ALU.add))
            dve.wait_ge(sem("gelu_sq"), 1)
            o.link(TS(T1[:, :, :], T1[:, :, :], 0.044715, 1.0, ALU.mult, ALU.add))
            TTN(T1[:, :, :], T1[:, :, :], GR, ALU.mult).then_inc(sem("gelu_in"), 1)
            dve.wait_ge(sem("gelu_tanh"), 1)
            o.link(STT(T1[:, :, :], T1[:, :, :], 1.0, GR, ALU.add, ALU.mult))
            STT(T1[:, :, :], T1[:, :, :], 0.5, XC[:, :, :], ALU.mult, ALU.mult).then_inc(sem("y_rnn"), 1)
            o.link(TS(PROJ[:, Q:Q + 8, :], PROJ[:, Q:Q + 8, :], HD ** -0.5, None, ALU.mult))
            dve.wait_ge(sem("yr_hi"), 1)
            TTN(YRL[:, :, :], T1[:, :, :], YRH[:, :, :].bitcast(f32), ALU.subtract).then_inc(sem("yr_lo"), 1)
            dve.wait_ge(sem("yr_lo"), 1)
            dve.wait_ge(sem("v_ready"), 1)
            dve.wait_ge(sem("kd_loaded"), 16 * 2 * KV)
            with o.loop(0, KV, 1 + 8 * 3) as j:
                o.mark(vec.tensor_copy(QS[:, :, :], PROJ[:, ds(j * 2 + Q, 2), :]))
                vec.tensor_copy(KS[:, :], chunk(KD, j)).then_inc(sem("a_staged"), 1)

                def peak(u):
                    x, b = u // 2, u % 2
                    n = (b + 1) * P
                    if u >= 2:
                        dve.wait_ge(sem("a_sink"), j * 8 + (u - 1))
                    dve.wait_ge(sem("a_scores"), j * 8 + (u + 1))
                    m = STAT[:, 0, b:b + 1]
                    o.link(vec.tensor_reduce(m, bank[b][:, 0:n], AX.X, ALU.max, negate=True))
                    TTN(m, m, SINK[:, 1, ds(j * 4 + x, 1)], ALU.min).then_inc(sem("a_max"), 1)

                def weigh(u):
                    x, b = u // 2, u % 2
                    n = (b + 1) * P
                    dve.wait_ge(sem("a_T"), j * 8 + (u + 1))
                    vec.tensor_copy(ET[b][:, 0:n], bank[2 + b][:, 0:n]).then_inc(sem("a_ET"), 1)
                    dve.wait_ge(sem("a_sink"), j * 8 + (u + 1))
                    o.link(TTN(STAT[:, 3, b:b + 1], STAT[:, 1, b:b + 1], STAT[:, 2, b:b + 1], ALU.add))
                    o.link(vec.reciprocal(STAT[:, 4, b:b + 1], STAT[:, 3, b:b + 1]))
                    dve.wait_ge(sem("a_pv"), j * 8 + (u + 1))
                    TS(OT[:, b, ds(j * 256 + x * HD, HD)], bank[4 + b][:, 0:HD], STAT[:, 4, b:b + 1], None,
                       ALU.mult).then_inc(sem("a_out"), 1)
                peak(0)
                for u in range(8):
                    if u < 7:
                        peak(u + 1)
                    weigh(u)
            dve.wait_ge(sem("ya_hi"), 1)
            TTN(YAL[:, :, :], OF[:, :, :], YAH[:, :, :].bitcast(f32), ALU.subtract).then_inc(sem("ya_lo"), 1)

            def post_wor(i, u):
                m = i * wor.U + u
                dve.wait_ge(evacuated, tile_end(wor, i, u))
                o.mark(TTN(T2[:, m, :], T2[:, m, :], PROJ[:, 28 + m, :], ALU.mult))

            def post_woa(i, u):
                m = i * woa.U + u
                dve.wait_ge(evacuated, tile_end(woa, i, u))
                o.link(TTN(T1[:, m, :], T1[:, m, :], PROJ[:, 36 + m, :], ALU.mult))
                o.link(TTN(T1[:, m, :], T1[:, m, :], T2[:, m, :], ALU.add))
                o.link(vec.tensor_copy(MGH[:, m, :], T1[:, m, :]))
                TTN(MGL[:, m, :], T1[:, m, :], MGH[:, m, :].bitcast(f32), ALU.subtract).then_inc(sem("merged"), 1)
            dve.wait_ge(sem("merge_gates"), 1)
            run_layer(dve, wor, lo_tile, post_wor)
            dve.wait_ge(mm_done, wor.n0 + 8)
            run_layer(dve, woa, lo_tile, post_woa)
            run_layer(dve, wout, lo_tile, lambda i, u: None)
            dve.wait_ge(sem("post_root"), 1)
            o.link(vec.reciprocal(RS[:, :], SD[:, :]))
            for c in range(DC):
                o.link(TTN(T1[:, c, :], T1[:, c, :], RS[:, :], ALU.mult))
                last = STT(XT[:, c, :], T1[:, c, :], ADV[:, 1, c:c + 1], XT[:, c, :], ALU.mult, ALU.add)
                if c < DC - 1:
                    o.mark(last)
            last.then_inc(sem("x_ready"), 1)

        phase(pool=pool, act=act, pe=pe, dve=dve)
        updates["whole"] += 1

    if "A" in phases:
        mixer()
    rw = Region(body0)
    W1 = rw("W1", [4, 2, 2 * FF])
    assert rw.o <= work0
    rw = Region(work0)
    W2 = rw("W2", [2, 4, D])
    B1 = rw("B1", [2 * FF])
    H2K = rw("H2K", [TT, D])
    ACC = rw("ACC", [TT, D])
    H2F = rw("H2F", [DC, S])
    PSEL = rw("PSEL", [TT, SLOTS])
    PGAT = rw("PGAT", [TT, 2 * SLOTS])
    PGT = rw("PGT", [S])
    XG = rw("XG", [DC, SLOTS])
    small_at = rw.o
    GLU = rw("GLU", [2 * S])
    LIN = rw("LIN", [2 * S])
    SIG = rw("SIG", [2 * S])
    AC = rw("AC", [4, P])
    AT = rw("AT", [4, P])
    YE = rw("YE", [512])
    NBI = rw("NBI", [3 * NE], i32)
    RANK = rw("RANK", [TT, NE])
    GAT = rw("GAT", [TT, NE])
    EH = rw("EH", [SLOTS])
    RKE = rw("RKE", [TT])
    GTE = rw("GTE", [TT])
    rs = Region(small_at)
    B2A = rs("B2A", [D])
    RTW = rs("RTW", [DC, NE])
    RTB = rs("RTB", [NE])
    IOE = rs("IOE", [NE])
    LG = rs("LG", [TT, NE])
    TOPV = rs("TOPV", [TT, 8])
    TOPI = rs("TOPI", [TT, 8], u32)
    TOPF = rs("TOPF", [TT, 8])
    EXV = rs("EXV", [TT, TOPK])
    GSC = rs("GSC", [8])
    MSK = rs("MSK", [TT, NE])
    ONEH = rs("ONEH", [TT, NE])
    NBF = rs("NBF", [6, NE])
    GTT = rs("GTT", [S])
    assert rs.o <= small_at + 12 * KB

    COMB = (2, 3, 4, 7)

    class Blocks:

        def __init__(self, eng, name):
            self.eng, self.reg = eng, eng.alloc_register(f"blocks_{name}")
            eng.reg_mov(self.reg, 1)

        def now(self):
            return self.eng.snap(self.reg, min_val=1, max_val=S // SLOTS * NE)

        def end(self):
            self.eng.reg_add(self.reg, self.reg, 1)

        def of(self, e):
            return self.eng.value_load(NBI[0:1, ds(e, 1)], min_val=1, max_val=S // SLOTS)

    def expert_loads(sp):
        w1 = A["moe_w1"][0].rearrange("e (q k p) n -> e q p k n", q=4, p=P)
        w2 = A["moe_w2"][0].rearrange("e (q k p) n -> e q p k n", q=2, p=P)

        def load(e, mm1_free=None, mm2_free=None):
            def at_e(w, q):
                if isinstance(e, int):
                    return w[e, q]
                return w[ds(e, 1), q].rearrange("a p k n -> (a p) k n")
            for q in range(4):
                if mm1_free is not None:
                    sp.wait_ge(sem("mm1_done"), mm1_free + q)
                sp.dma_start(W1[:, q], at_e(w1, q)).then_inc(sem(f"w1_loaded{q}"), 16)
            for q in range(2):
                if mm2_free is not None:
                    sp.wait_ge(sem("mm2_done"), mm2_free + q)
                sp.dma_start(W2[:, q], at_e(w2, q)).then_inc(sem(f"w2_loaded{q}"), 16)
        if "A" in phases:
            sp.wait_ge(mm_done, by_name["wout"].n0 + 8)
        else:
            sp.wait_ge(sem("ada_ready"), 5)
        sp.dma_start(B1[0:NE, :], A["moe_b1"][0]).then_inc(sem("b1_loaded"), 16)
        load(0)
        sp.wait_ge(sem("blocks_ready"), 1)
        with sp.Fori(1, NE) as e:
            f1 = sp.value_load(NBI[0:1, ds(e + (NE - 1), 1)], min_val=1, max_val=4 * S // SLOTS * NE)
            f2 = sp.value_load(NBI[0:1, ds(e + (2 * NE - 1), 1)], min_val=1, max_val=2 * S // SLOTS * NE)
            load(e, f1, f2)

    def experts():
        norm = Norm(H2F, lambda c: ADV[:, 2, c:c + 1], lambda c: ADA[:, 24 + c:25 + c], keep=True)
        kx = updates["whole"]

        def pool(pool):
            if kx:
                pool.wait_ge(sem("x_ready"), kx)
            else:
                pool.wait_ge(sem("ada_ready"), 5)
            pool.dma_start(RTW[:, :, :], A["router_w"]).then_inc(sem("router_loaded"), 16)
            pool.dma_start(RTB[:, :], A["router_b"]).then_inc(sem("router_loaded"), 16)
            pool.dma_start(B2A[0:NE, :], A["moe_b2"][0]).then_inc(sem("router_loaded"), 16)
            pool.dma_start(IOE[:, :], A["expert_no"]).then_inc(sem("router_loaded"), 16)

        def act(act):
            o = own["act"]
            norm.act(act, o)
            for m in range(4):
                act.wait_ge(sem("h_T"), m + 1)
                act_f(H2K[:, m // 2, 512 * (m % 2):512 * (m % 2 + 1)], bank[m][:, :], ACT.Copy).then_inc(sem("h_ready"), 1)
            for tt in range(TT):
                act.wait_ge(sem("top_ready"), tt + 1)
                act_f(EXV[:, tt, :], TOPV[:, tt, 0:TOPK], ACT.Exp, bias=GSC[:, tt:tt + 1],
                      accum_out=GSC[:, 2 + tt:3 + tt]).then_inc(sem("top_exp"), 1)
            act.wait_ge(sem("gates_T"), 1)
            act_f(GTT[0:NE, :], bank[7][0:NE, 0:S], ACT.Copy).then_inc(sem("gt_ready"), 1)
            for m in range(4):
                act.wait_ge(sem("b2_mm"), m + 1)
                act_f(ACC[:, m // 2, 512 * (m % 2):512 * (m % 2 + 1)], bank[m][:, :], ACT.Copy).then_inc(sem("acc_ready"), 1)
            act_f(YE[:, :], SM[:, :], ACT.Copy, scale=0.0).then_inc(sem("y_ready"), 1)
            blocks = Blocks(act, "act")
            act.wait_ge(sem("blocks_ready"), 1)
            with act.Fori(0, NE) as e:
                with act.Fori(0, blocks.of(e)):
                    d = blocks.now()
                    act.wait_ge(sem("xg_mm"), d)
                    act_f(XG[:, :, :], bank[4][:, :].rearrange("p (k s) -> p k s", k=DC), ACT.Copy).then_inc(sem("xg_ready"), 1)
                    act.wait_ge(sem("glu_ready"), d)
                    act_f(SIG[:, :], GLU[:, :], ACT.Sigmoid, scale=1.702).then_inc(sem("sig_ready"), 1)
                    act.wait_ge(sem("comb_mm"), d * 4)
                    act.wait_ge(sem("pgt_mm"), d)
                    act_f(PGT[:, :], bank[6][:, 0:S], ACT.Copy).then_inc(sem("pgt_ready"), 1)
                    act.wait_ge(sem("at_mm"), d)
                    act_f(AT[:, :, :], bank[5][:, :].rearrange("p (k s) -> p k s", k=4), ACT.Copy).then_inc(sem("at_ready"), 1)
                    act.wait_ge(sem("mm2_done"), d * 2)
                    act_f(YE[:, :], bank[6][:, :], ACT.Copy).then_inc(sem("y_ready"), 1)
                    blocks.end()
            act.wait_ge(sem("acc_done"), 1)
            for tt in range(TT):
                act_f(H2F[:, 4 * tt:4 * tt + 4, :], ACC[:, tt, :].rearrange("p (a s) -> p a s", a=4), ACT.Square,
                      accum_out=STAT[:, 5, tt:tt + 1]).then_inc(sem("ff_sq"), 1)
            act.wait_ge(sem("ff_sq"), 2)
            act_f(STAT[:, 6, :], STAT[:, 5, :], ACT.Sqrt, scale=1.0 / D, bias=EPSC[:, 0:1]).then_inc(sem("ff_root"), 1)

        def pe(pe):
            norm.pe(pe)
            pe.wait_ge(sem("kept"), DC)
            for m in range(4):
                for c in range(4):
                    k = 4 * (m % 2) + c
                    last = nc.tensor.transpose(bank[m][:, c * P:(c + 1) * P],
                                               H2F[:, k, (m // 2) * P:(m // 2 + 1) * P], IDENT)
                last.then_inc(sem("h_T"), 1)
            pe.wait_ge(sem("router_loaded"), 64)
            for tt in range(TT):
                for k in range(DC):
                    last = nc.tensor.matmul(bank[4][:, tt * NE:(tt + 1) * NE], H2F[:, k, tt * P:(tt + 1) * P],
                                            RTW[:, k, :], start=k == 0, stop=k == DC - 1)
            last.then_inc(sem("logits_mm"), 1)
            pe.wait_ge(sem("mask_ready"), 1)
            nc.tensor.matmul(bank[5][:, 0:NE], BEFORE, MSK[:, 0, :], start=True, stop=True)
            nc.tensor.matmul(bank[5][:, NE:2 * NE], BEFORE, MSK[:, 1, :], start=True, stop=False)
            nc.tensor.matmul(bank[5][:, NE:2 * NE], ONE[:, :], MSK[:, 0, :], start=False, stop=True).then_inc(sem("rank_mm"), 1)
            nc.tensor.matmul(bank[6][0:1, 0:NE], ONE[:, 0:1], MSK[:, 0, :], start=True, stop=False)
            nc.tensor.matmul(bank[6][0:1, 0:NE], ONE[:, 0:1], MSK[:, 1, :], start=False, stop=True).then_inc(sem("count_mm"), 1)
            pe.wait_ge(sem("gat_ready"), 1)
            for tt in range(TT):
                last = nc.tensor.transpose(bank[7][0:NE, tt * P:(tt + 1) * P], GAT[:, tt, :], IDENT)
            last.then_inc(sem("gates_T"), 1)
            pe.wait_ge(sem("gt_ready"), 1)
            pe.wait_ge(sem("h_ready"), 4)
            for m in range(4):
                nc.tensor.matmul(bank[m][:, :], GTT[0:NE, (m // 2) * P:(m // 2 + 1) * P],
                                 B2A[0:NE, 512 * (m % 2):512 * (m % 2 + 1)], start=True, stop=True).then_inc(sem("b2_mm"), 1)
            pe.wait_ge(sem("acc_ready"), 4)
            blocks = Blocks(pe, "pe")

            def combine(d):
                pe.wait_ge(sem("y_ready"), d)
                pe.wait_ge(sem("pgt_ready"), d)
                for m in range(4):
                    tt, g = m // 2, m % 2
                    nc.tensor.matmul(bank[COMB[m]][:, :], PGT[64 * g:64 * g + 64, tt * P:(tt + 1) * P],
                                     YE[64 * g:64 * g + 64, :], start=True, stop=True).then_inc(sem("comb_mm"), 1)
            pe.wait_ge(sem("blocks_ready"), 1)
            pe.wait_ge(sem("b1_loaded"), 16)
            with pe.Fori(0, NE) as e:
                pe.wait_ge(sem("e_taken"), e + 1)
                with pe.Fori(0, blocks.of(e)):
                    d = blocks.now()
                    pe.wait_ge(sem("p_ready"), d)
                    for k in range(DC):
                        for tt in range(TT):
                            last = nc.tensor.matmul(bank[4][:, k * SLOTS:(k + 1) * SLOTS], H2K[:, tt, k * P:(k + 1) * P],
                                                    PSEL[:, tt, :], start=tt == 0, stop=tt == TT - 1)
                    last.then_inc(sem("xg_mm"), 1)
                    for j in range(2):
                        for g in range(2):
                            nc.tensor.matmul(bank[j][64 * g:64 * g + 64, :], EH[0:NE, :],
                                             B1[0:NE, 1024 * g + 512 * j:1024 * g + 512 * (j + 1)], start=True, stop=False)
                    pe.wait_ge(sem("xg_ready"), d)
                    for q in range(4):
                        pe.wait_ge(sem(f"w1_loaded{q}"), e * 16 + 16)
                        for k in range(2):
                            for j in range(2):
                                for g in range(2):
                                    last = nc.tensor.matmul(bank[j][64 * g:64 * g + 64, :], XG[:, 2 * q + k, :],
                                                            W1[:, q, k, 1024 * g + 512 * j:1024 * g + 512 * (j + 1)],
                                                            start=False, stop=q == 3 and k == 1)
                        last.then_inc(sem("mm1_done"), 1)
                    combine(d)
                    for tt in range(TT):
                        last = nc.tensor.transpose(bank[6][:, tt * P:(tt + 1) * P], PGAT[:, tt, :], IDENT)
                    last.then_inc(sem("pgt_mm"), 1)
                    pe.wait_ge(sem("ac_ready"), d)
                    for b in range(4):
                        last = nc.tensor.transpose(bank[5][:, b * P:(b + 1) * P], AC[:, b, :], IDENT)
                    last.then_inc(sem("at_mm"), 1)
                    pe.wait_ge(sem("at_ready"), d)
                    for q in range(2):
                        pe.wait_ge(sem(f"w2_loaded{q}"), e * 16 + 16)
                        for b in range(4):
                            for g in range(2):
                                last = nc.tensor.matmul(bank[6][64 * g:64 * g + 64, :], AT[:, b, 64 * q:64 * q + 64],
                                                        W2[:, q, b, 512 * g:512 * (g + 1)],
                                                        start=q == 0 and b == 0, stop=q == 1 and b == 3)
                        last.then_inc(sem("mm2_done"), 1)
                    blocks.end()
            d = blocks.now()
            pe.wait_ge(sem("p_ready"), d)
            combine(d)
            pe.wait_ge(sem("ff_scaled"), 2)
            for m in range(4):
                for c in range(2):
                    for tt in range(TT):
                        last = nc.tensor.transpose(bank[m][:, c * S + tt * P:c * S + (tt + 1) * P],
                                                   ACC[:, tt, (2 * m + c) * P:(2 * m + c + 1) * P], IDENT)
                last.then_inc(sem("ff_T"), 1)

        def dve(dve):
            o = own["dve"]
            norm.dve(dve, o)
            dve.wait_ge(sem("router_loaded"), 64)
            dve.wait_ge(sem("logits_mm"), 1)
            for tt in range(TT):
                o.link(TTN(LG[:, tt, :], bank[4][:, tt * NE:(tt + 1) * NE], RTB[:, :], ALU.add))
                o.link(vec.max(TOPV[:, tt, :], LG[:, tt, :]))
                o.mark(vec.max_index(TOPI[:, tt, :], TOPV[:, tt, :], LG[:, tt, :]))
                TS(GSC[:, tt:tt + 1], TOPV[:, tt, 0:1], -1.0, None, ALU.mult).then_inc(sem("top_ready"), 1)
            o.wait()
            for tt in range(TT):
                o.link(vec.tensor_copy(TOPF[:, tt, :], TOPI[:, tt, :]))
                dve.wait_ge(sem("top_exp"), tt + 1)
                o.link(vec.reciprocal(GSC[:, 4 + tt:5 + tt], GSC[:, 2 + tt:3 + tt]))
                o.link(TS(EXV[:, tt, :], EXV[:, tt, :], GSC[:, 4 + tt:5 + tt], None, ALU.mult))
                for k in range(TOPK):
                    first = k == 0
                    o.link(TS(ONEH[:, tt, :], IOE[:, :], TOPF[:, tt, k:k + 1], None, ALU.is_equal))
                    if first:
                        o.mark(vec.tensor_copy(MSK[:, tt, :], ONEH[:, tt, :]))
                        o.link(TS(GAT[:, tt, :], ONEH[:, tt, :], EXV[:, tt, 0:1], None, ALU.mult))
                    else:
                        o.mark(TTN(MSK[:, tt, :], MSK[:, tt, :], ONEH[:, tt, :], ALU.add))
                        o.link(STT(GAT[:, tt, :], ONEH[:, tt, :], EXV[:, tt, k:k + 1], GAT[:, tt, :], ALU.mult, ALU.add))
            TS(ONEH[:, :, :], MSK[:, :, :], 4096.0, -4096.0, ALU.mult, ALU.add).then_inc(sem("mask_ready"), 1)
            dve.wait_ge(sem("mask_ready"), 1)
            dve.wait_ge(sem("rank_mm"), 1)
            TTN(RANK[:, :, :], bank[5][:, 0:TT * NE].rearrange("p (t e) -> p t e", t=TT), ONEH[:, :, :],
                ALU.add).then_inc(sem("gat_ready"), 1)
            dve.wait_ge(sem("count_mm"), 1)
            cnt = NBF[0:1, 0, :]
            o.link(vec.tensor_copy(cnt, bank[6][0:1, 0:NE]))
            o.link(TS(NBF[0:1, 1, :], cnt, float(SLOTS), 1.0, ALU.is_gt, ALU.add))
            for b in range(2, S // SLOTS):
                o.link(TS(NBF[0:1, 2, :], cnt, float(b * SLOTS), None, ALU.is_gt))
                o.link(TTN(NBF[0:1, 1, :], NBF[0:1, 1, :], NBF[0:1, 2, :], ALU.add))
            o.link(vec.memset(NBF[0:1, 2, :], 1.0))
            o.link(vec.tensor_tensor_scan(NBF[0:1, 5, :], NBF[0:1, 2, :], NBF[0:1, 1, :], 0.0, ALU.mult, ALU.add))
            o.link(TS(NBF[0:1, 2, :], NBF[0:1, 5, :], 4.0, -3.0, ALU.mult, ALU.add))
            o.link(TS(NBF[0:1, 3, :], NBF[0:1, 5, :], 2.0, -1.0, ALU.mult, ALU.add))
            vec.tensor_copy(NBI[0:1, :], NBF[0:1, 1:4, :].rearrange("p a e -> p (a e)")).then_inc(sem("blocks_ready"), 1)
            dve.wait_ge(sem("blocks_ready"), 1)
            dve.wait_ge(sem("acc_ready"), 4)
            vec.memset(PGT[:, :], 0.0).then_inc(sem("pgt_ready"), 1)
            blocks = Blocks(dve, "dve")

            def add_sums(d):
                for m in range(4):
                    tt, g = m // 2, m % 2
                    dve.wait_ge(sem("comb_mm"), d * 4 + (m - 3))
                    a = ACC[:, tt, 512 * g:512 * (g + 1)]
                    TTN(a, a, bank[COMB[m]][:, :], ALU.add).then_inc(sem("added"), 1)
                dve.wait_ge(sem("added"), d * 4)
            with dve.Fori(0, NE) as e:
                vec.tensor_copy(RKE[:, :], RANK[:, :, ds(e, 1)].rearrange("p t a -> p (t a)"))
                vec.tensor_copy(GTE[:, :], GAT[:, :, ds(e, 1)].rearrange("p t a -> p (t a)"))
                vec.tensor_copy(EH[0:NE, :], IDENT[0:NE, ds(e, 1)].to_broadcast([NE, SLOTS])).then_inc(sem("e_taken"), 1)
                dve.wait_ge(sem("e_taken"), e + 1)
                with dve.Fori(0, blocks.of(e)):
                    d = blocks.now()
                    for tt in range(TT):
                        TS(PSEL[:, tt, :], SLOT[:, 0:SLOTS], RKE[:, tt:tt + 1], None, ALU.is_equal)
                        last = TS(PGAT[:, tt, :], SLOT[:, :], RKE[:, tt:tt + 1], GTE[:, tt:tt + 1], ALU.is_equal, ALU.mult)
                    last.then_inc(sem("p_ready"), 1)
                    dve.wait_ge(sem("p_ready"), d)
                    TS(RKE[:, :], RKE[:, :], -float(SLOTS), None, ALU.add).then_inc(sem("rk_next"), 1)
                    dve.wait_ge(sem("mm1_done"), d * 4)
                    pairs = PS[:, 0:1024].rearrange("p (n a) -> p n a", a=2)
                    TS(GLU[:, :], pairs[:, :, 0], 7.0, None, ALU.min).then_inc(sem("glu_ready"), 1)
                    TS(LIN[:, :], pairs[:, :, 1], -7.0, 7.0, ALU.max, ALU.min).then_inc(sem("lin_ready"), 1)
                    dve.wait_ge(sem("glu_ready"), d)
                    dve.wait_ge(sem("lin_ready"), d)
                    STT(LIN[:, :], LIN[:, :], 1.0, GLU[:, :], ALU.add, ALU.mult).then_inc(sem("lin_glu"), 1)
                    dve.wait_ge(sem("lin_glu"), d)
                    dve.wait_ge(sem("sig_ready"), d)
                    TTN(AC[:, :, :].rearrange("p a b -> p (a b)"), LIN[:, :], SIG[:, :], ALU.mult).then_inc(sem("ac_ready"), 1)
                    add_sums(d)
                    dve.wait_ge(sem("rk_next"), d)
                    dve.wait_ge(sem("xg_mm"), d)
                    dve.wait_ge(sem("pgt_mm"), d)
                    blocks.end()
            d = blocks.now()
            vec.memset(STAT[:, 5, :], 0.0).then_inc(sem("p_ready"), 1)
            add_sums(d)
            vec.memset(STAT[:, 5, :], 0.0).then_inc(sem("acc_done"), 1)
            dve.wait_ge(sem("ff_root"), 1)
            o.link(vec.reciprocal(STAT[:, 7, :], STAT[:, 6, :]))
            for tt in range(TT):
                TS(ACC[:, tt, :], ACC[:, tt, :], STAT[:, 7, tt:tt + 1], None, ALU.mult).then_inc(sem("ff_scaled"), 1)
            for c in range(DC):
                dve.wait_ge(sem("ff_T"), c // 2 + 1)
                last = STT(XT[:, c, :], bank[c // 2][:, (c % 2) * S:(c % 2 + 1) * S], ADV[:, 3, c:c + 1], XT[:, c, :],
                           ALU.mult, ALU.add)
            last.then_inc(sem("x_ready"), 1)
        phase(pool=pool, act=act, pe=pe, dve=dve)
        updates["whole"] += 1

    if "B" in phases:
        experts()
    XN = Region(work0)("XN", [DC, S])

    def split_into(o, dst_hi, dst_lo, src, name):
        o.link(vec.tensor_copy(dst_hi, src))
        TTN(dst_lo, src, dst_hi.bitcast(f32), ALU.subtract).then_inc(sem(name), 1)

    class Update:

        def __init__(self, L, DX, then):
            self.L, self.DX, self.then, self.base = L, DX, then, updates["chunks"]
            updates["chunks"] += DC

        def square(self, act, m):
            if self.then is not None:
                act.wait_ge(sem("added_x"), self.base + m + 1)
                self.then.square(act, m)

        def act(self, act, scale=1.0):
            def ev(i, u):
                m = i * self.L.U + u
                act.wait_ge(mm_done, tile_end(self.L, i, u))
                act_f(self.DX[:, m, :], tile_bank(self.L, u), ACT.Copy, scale=scale).then_inc(evacuated, 1)
                if m:
                    self.square(act, m - 1)
            run_layer(act, self.L, hi_tile, ev)
            self.square(act, DC - 1)

        def dve(self, dve):
            def post(i, u):
                m = i * self.L.U + u
                dve.wait_ge(evacuated, tile_end(self.L, i, u))
                TTN(XT[:, m, :], XT[:, m, :], self.DX[:, m, :], ALU.add).then_inc(sem("added_x"), 1)
            run_layer(dve, self.L, lo_tile, post)

        def pe(self, pe, xh, xl, feed=None):
            def mean(i, u):
                self.then.add_mean(pe, i * self.L.U + u)
            products(pe, self.L, xh, xl, behind=mean if self.then is not None else None, feed=feed)

    ffn_count = [0]

    def ffn(tag, norm, then):
        rg = Region(work0)
        GATE = rg(f"GATE{tag}", [FC, S])
        MIH = rg(f"MIH{tag}", [FC, S], f32r)
        MIL = rg(f"MIL{tag}", [FC, S], f32r)
        UP = rg(f"UP{tag}", [4, S])
        DX = rg(f"DX{tag}", [DC, S])
        gate, up, down = (by_name[f"{x}{tag}"] for x in ("gate", "up", "down"))
        update = Update(down, DX, then)
        turn = ffn_count[0]
        ffn_count[0] += 1

        def act(act):
            norm.act(act, own["act"])

            def ev_gate(i, u):
                act.wait_ge(mm_done, tile_end(gate, i, u))
                act_f(chunk(GATE, i * gate.U + u), tile_bank(gate, u), ACT.Silu).then_inc(evacuated, 1)

            def ev_up(i, u):
                act.wait_ge(mm_done, tile_end(up, i, u))
                act_f(UP[:, u % 4, :], tile_bank(up, u), ACT.Copy).then_inc(evacuated, 1)

            run_layer(act, gate, hi_tile, ev_gate)
            run_layer(act, up, hi_tile, ev_up)
            update.act(act, 0.5)

        def pe(pe):
            norm.pe(pe)
            products(pe, gate, HNH, HNL, feed=norm.feed)
            products(pe, up, HNH, HNL)
            update.pe(pe, MIH, MIL, feed=lambda pe, k: pe.wait_ge(sem("mid_done"), turn * FC + k + 1))

        def dve(dve):
            o = own["dve"]
            norm.dve(dve, o)

            def post_up(i, u):
                dve.wait_ge(evacuated, tile_end(up, i, u))
                m = i * up.U + u
                g = chunk(GATE, m)
                TTN(g, g, UP[:, u % 4, :], ALU.mult).then_inc(sem("mid_mult"), 1)
                dve.wait_ge(sem("mid_mult"), turn * FC + m + 1)
                vec.tensor_copy(chunk(MIH, m), g).then_inc(sem("mid_hi"), 1)
                dve.wait_ge(sem("mid_hi"), turn * FC + m + 1)
                TTN(chunk(MIL, m), g, chunk(MIH, m).bitcast(f32), ALU.subtract).then_inc(sem("mid_done"), 1)

            run_layer(dve, gate, lo_tile, lambda i, u: None)
            run_layer(dve, up, lo_tile, post_up)
            update.dve(dve)
        phase(act=act, pe=pe, dve=dve)

    def conv_mixer(norm, then):
        rg = Region(work0)
        C = rg("CC", [DC, S])
        VP = rg("VP", [DC, S + 2])
        B = rg("CB", [DC, S])
        CT = rg("CT", [DC, S])
        OH, OL = rg("COH", [DC, S], f32r), rg("COL", [DC, S], f32r)
        DX = rg("DXC", [DC, S])
        U_ = rg("CUU", [4, S])
        cu, cb, co = (by_name[x] for x in ("conv_cu", "conv_b", "conv_out"))
        update = Update(co, DX, then)

        def act(act):
            norm.act(act, own["act"])

            def ev_cu(i, u):
                m = i * cu.U + u
                act.wait_ge(mm_done, tile_end(cu, i, u))
                if m >= 12:
                    act.wait_ge(sem("cv_in"), m - 11)
                dst = C[:, m, :] if m < DC else U_[:, m % 4, :]
                act_f(dst, tile_bank(cu, u), ACT.Copy).then_inc(evacuated, 1)

            def ev(L, dst):
                def f(i, u):
                    act.wait_ge(mm_done, tile_end(L, i, u))
                    act_f(dst[:, i * L.U + u, :], tile_bank(L, u), ACT.Copy).then_inc(evacuated, 1)
                return f
            run_layer(act, cu, hi_tile, ev_cu)
            run_layer(act, cb, hi_tile, ev(cb, B))
            update.act(act)

        def pe(pe):
            norm.pe(pe)
            products(pe, cu, HNH, HNL, feed=norm.feed)
            products(pe, cb, HNH, HNL)
            update.pe(pe, OH, OL, feed=lambda pe, k: pe.wait_ge(sem("conv_split"), k + 1))

        def dve(dve):
            o = own["dve"]
            norm.dve(dve, o)

            def post_cu(i, u):
                m = i * cu.U + u - DC
                if m < 0:
                    return
                dve.wait_ge(evacuated, tile_end(cu, i, u))
                if m == 0:
                    o.link(vec.memset(VP[:, :, 0:2], 0.0))
                v = VP[:, m, :]
                TTN(v[:, 2:S + 2], C[:, m, :], U_[:, m % 4, :], ALU.mult).then_inc(sem("cv_in"), 1)
                dve.wait_ge(sem("cv_in"), m + 1)
                w = [col("conv_w_2", lag * DC + m) for lag in range(CONV_W2)]
                o.link(TS(CT[:, m, :], v[:, 2:S + 2], w[0], None, ALU.mult))
                o.link(STT(CT[:, m, :], v[:, 1:S + 1], w[1], CT[:, m, :], ALU.mult, ALU.add))
                o.link(STT(CT[:, m, :], v[:, 0:S], w[2], CT[:, m, :], ALU.mult, ALU.add))

            def post_b(i, u):
                m = i * cb.U + u
                dve.wait_ge(evacuated, tile_end(cb, i, u))
                o.link(TTN(CT[:, m, :], CT[:, m, :], B[:, m, :], ALU.mult))
                split_into(o, OH[:, m, :], OL[:, m, :], CT[:, m, :], "conv_split")

            run_layer(dve, cu, lo_tile, post_cu)
            run_layer(dve, cb, lo_tile, post_b)
            update.dve(dve)
        phase(act=act, pe=pe, dve=dve)

    def attention_mixer(norm, then):
        rg = Region(work0)
        QK = rg("QK", [2 * N_GROUPS, DC, S])
        VV = rg("VV", [N_GROUPS, TT, D])
        stage = rg.o
        QRAW = [rg(f"QRAW{i}", [S]) for i in range(4)]
        QSQ = [rg(f"QSQ{i}", [S]) for i in range(2)]
        QNR = [rg(f"QNR{i}", [S]) for i in range(4)]
        QST = rg("QST", [4, 4])
        rh = Region(hn0)
        QS = [rh(f"QS{i}", [N_GROUPS, S]) for i in range(2)]
        KS = [rh(f"KS{i}", [N_GROUPS, S]) for i in range(2)]
        assert rh.o <= work0
        rs = Region(stage)
        ES = [rs(f"ES{i}", [N_GROUPS * S]) for i in range(2)]
        ETX = [rs(f"ETX{i}", [N_GROUPS * S]) for i in range(2)]
        UB = [Region(raw0 + (i * FC + 2 * DC) * P * 4)(f"UB{i}", [N_GROUPS, S]) for i in range(4)]
        assert (FC - 2 * DC) * P >= N_GROUPS * S
        OTB = [Region(body0 + 16 * KB)("OT0", [D]), Region(body0 + 40 * KB)("OT1", [D])]
        ORD = Region(body0 + 20 * KB)("ORD", [2 * N_GROUPS, P])
        OX = Region(work0)("OX", [DC, S])
        OXH = Region(work0 + 8 * KB)("OXH", [DC, S], f32r)
        OXL = Region(work0 + 16 * KB)("OXL", [DC, S], f32r)
        DX = Region(work0 + 24 * KB)("DXT", [DC, S])
        qk, vl, ao = (by_name[x] for x in ("qk", "v", "attn_out"))
        update = Update(ao, DX, then)

        TURN = 4
        NU = 2 * TURN

        def pool(pool):
            pool.wait_ge(sem("hn_dead"), 1)
            with pool.Fori(0, HEADS // TURN) as c:
                for x in range(TURN):
                    pool.wait_ge(sem("ub_free"), c * TURN + (x + 1))
                    for g in range(N_GROUPS):
                        flat = bias_rows.rearrange("g h j -> (g h j)")
                        row = flat[ds(c * (TURN * 384) + (g * HEADS + x) * 384, 384)]
                        src = bass.AP(tensor=row.tensor, offset=row.offset, ap=[[1, P], [1, S]])
                        pool.dma_start(UB[x][:, g, :], src).then_inc(sem(f"ub_loaded{x}"), 16)

        def act(act):
            o = own["act"]
            norm.act(act, o)

            def root(i, u):
                t = i * qk.U + u
                act.wait_ge(sem("q_summed"), t + 1)
                st = QST[:, u % 4, :]
                act_f(st, st, ACT.Sqrt, scale=1.0 / HD, bias=EPSC[:, 0:1]).then_inc(sem("q_root"), 1)

            def take(i, u):
                act.wait_ge(sem("q_T"), i * qk.U + (u + 1))
                m, tt = u // 2, u % 2
                dst = QK[:, ds(i, 1), 2 * m:2 * m + 2, tt * P:(tt + 1) * P] if not isinstance(i, int) else \
                    QK[:, i:i + 1, 2 * m:2 * m + 2, tt * P:(tt + 1) * P]
                gcol = QKG[:, ds(i, 1)] if not isinstance(i, int) else QKG[:, i:i + 1]
                act_f(dst.rearrange("p a c n -> p (a c) n"), bank[4 + u % 2][:, 0:S].rearrange("p (c n) -> p c n", c=2),
                      ACT.Copy, scale=gcol).then_inc(sem("q_taken"), 1)

            def ev_qk(i, u):
                n = tile_end(qk, i, u)
                act.wait_ge(mm_done, n)
                r = QRAW[u % 4]
                act_f(r[:, :], tile_bank(qk, u), ACT.Copy).then_inc(evacuated, 1)
                act.wait_ge(evacuated, n)
                act_f(QSQ[u % 2][:, :], r[:, :], ACT.Square).then_inc(sem("q_sq"), 1)
                if not isinstance(i, int) or i * qk.U + u >= 1:
                    root(*back(qk, i, u, 1))
                if not isinstance(i, int) or i * qk.U + u >= 3:
                    take(*back(qk, i, u, 3))

            def ev_v(i, u):
                act.wait_ge(mm_done, tile_end(vl, i, u))
                m = u // 2
                dst = VV[:, ds(i, 1), u % 2, m * S:(m + 1) * S].rearrange("p a n -> p (a n)") if not isinstance(i, int) \
                    else VV[:, i, u % 2, m * S:(m + 1) * S]
                act_f(dst, tile_bank(vl, u), ACT.Copy).then_inc(evacuated, 1)
            act.wait_ge(sem("gains_ready"), 6)
            run_layer(act, qk, hi_tile, ev_qk, peel=qk.U)
            root(*back(qk, qk.T // qk.U, 0, 1))
            for k in (3, 2, 1):
                take(*back(qk, qk.T // qk.U, 0, k))
            run_layer(act, vl, hi_tile, ev_v)
            with act.Fori(0, HEADS // TURN) as c:
                for u in range(NU):
                    b = u % 2
                    n = N_GROUPS * (b + 1) * P
                    act.wait_ge(sem("b_max"), c * NU + (u + 1))
                    act_f(ES[b][:, 0:n], ES[b][:, 0:n], ACT.Exp, bias=STAT[:, 0, b:b + 1],
                          accum_out=STAT[:, 1, b:b + 1]).then_inc(sem("b_exp"), 1)
                    if b:
                        act.wait_ge(sem("b_T"), c * NU + (u + 1))
                        act_f(ETX[b][:, 512:768], bank[5][:, 0:2 * P], ACT.Copy).then_inc(sem("b_ET_act"), 1)
            for m in range(4):
                act.wait_ge(sem("x_T"), m + 1)
                act_f(OX[:, 2 * m:2 * m + 2, :], bank[m][:, :].rearrange("p (a n) -> p a n", a=2), ACT.Copy).then_inc(sem("x_full"), 1)
            act.wait_ge(sem("x_full"), 4)
            act_f(OXH[:, :, :], OX[:, :, :], ACT.Copy).then_inc(sem("ox_hi"), 1)

            update.act(act)

        def pe(pe):
            norm.pe(pe)

            def transposes(i, u):
                t = i * qk.U + u
                pe.wait_ge(sem("q_normed"), t + 1)
                if not isinstance(t, int) or t >= 2:
                    pe.wait_ge(sem("q_taken"), t - 1)
                for c in range(2):
                    last = nc.tensor.matmul(bank[4 + u % 2][:, c * P:(c + 1) * P], QNR[u % 4][:, c * P:(c + 1) * P],
                                            chunk(ORD, i), start=True, stop=True)
                last.then_inc(sem("q_T"), 1)
            pe.wait_ge(sem("order_ready"), 2 * N_GROUPS)
            products(pe, qk, HNH, HNL, behind=transposes, feed=norm.feed)
            products(pe, vl, HNH, HNL)
            pe.wait_ge(evacuated, vl.n0 + vl.T)

            def scores(c, u):
                x, b = u // 2, u % 2
                n = (b + 1) * P
                h = slice(64 * (x % 2), 64 * (x % 2) + 64)
                if u % 4 == 0:
                    pe.wait_ge(sem("b_staged"), c * 2 + (u // 4 + 1))
                for g in range(N_GROUPS):
                    o = PS[:, b * 1024 + g * n:b * 1024 + (g + 1) * n]
                    last = nc.tensor.matmul(o, QS[u // 4][h, g, b * P:(b + 1) * P], KS[u // 4][h, g, 0:n], start=True, stop=True)
                last.then_inc(sem("b_scores"), 1)

            def turn_keys(c, u):
                b = u % 2
                pe.wait_ge(sem("b_exp"), c * NU + (u + 1))
                for j in range(N_GROUPS * (b + 1)):
                    last = nc.tensor.transpose(PS[:, 2048 + j * P:2048 + (j + 1) * P], ES[b][:, j * P:(j + 1) * P], IDENT)
                last.then_inc(sem("b_T"), 1)

            def weigh(c, u, ahead):
                x, b = u // 2, u % 2
                nk = b + 1
                pe.wait_ge(sem("b_ET"), c * NU + (u + 1))
                if b:
                    pe.wait_ge(sem("b_ET_act"), c * TURN + (x + 1))
                if ahead is not None:
                    turn_keys(*ahead)
                for j in range(N_GROUPS * nk):
                    g, kb = j // nk, j % nk
                    last = nc.tensor.matmul(bank[6 + b][:, 0:HD], ETX[b][:, j * P:(j + 1) * P],
                                            VV[:, g, kb, ds(c * (TURN * HD) + x * HD, HD)], start=j == 0,
                                            stop=j == N_GROUPS * nk - 1)
                last.then_inc(sem("b_pv"), 1)

            def turn(c, last):
                for u in range(NU):
                    if not (last and u >= NU - 2):
                        scores(c + (u + 2) // NU, (u + 2) % NU)
                    weigh(c, u, None if last and u == NU - 1 else (c + (u + 1) // NU, (u + 1) % NU))
            scores(0, 0)
            scores(0, 1)
            turn_keys(0, 0)
            with pe.Fori(0, HEADS // TURN - 1) as c:
                turn(c, False)
            turn(HEADS // TURN - 1, True)
            pe.wait_ge(sem("b_out"), 2 * HEADS)
            for m in range(4):
                for c in range(2):
                    for tt in range(TT):
                        last = nc.tensor.matmul(bank[m][:, c * S + tt * P:c * S + (tt + 1) * P],
                                                OTB[tt][:, (2 * m + c) * P:(2 * m + c + 1) * P], FLIP, start=True, stop=True)
                last.then_inc(sem("x_T"), 1)
            pe.wait_ge(sem("x_full"), 4)
            pe.wait_ge(sem("ox_lo"), 1)
            update.pe(pe, OXH, OXL)

        def dve(dve):
            o = own["dve"]
            norm.dve(dve, o)
            g0 = COL["attn_q_gain_2"]
            for g in range(N_GROUPS):
                TS(QKG[:, 2 * g:2 * g + 1], PRM[:, g0 + g:g0 + g + 1], HD ** -0.5, None, ALU.mult).then_inc(sem("gains_ready"), 1)
                vec.tensor_copy(QKG[:, 2 * g + 1:2 * g + 2], PRM[:, g0 + 3 + g:g0 + 4 + g]).then_inc(sem("gains_ready"), 1)

            for i in range(2 * N_GROUPS):
                vec.tensor_copy(ORD[:, i, :], (FLIP, IDENT)[i % 2]).then_inc(sem("order_ready"), 1)

            def normalise(i, u):
                t = i * qk.U + u
                dve.wait_ge(sem("q_root"), t + 1)
                st = QST[:, u % 4, :]
                vec.reciprocal(st, st).then_inc(sem("q_recip"), 1)
                dve.wait_ge(sem("q_recip"), t + 1)
                TTN(QNR[u % 4][:, :].rearrange("p (h d) -> p h d", h=4), QRAW[u % 4][:, :].rearrange("p (h d) -> p h d", h=4),
                    st.rearrange("p (h a) -> p h a", a=1).to_broadcast([P, 4, HD]), ALU.mult).then_inc(sem("q_normed"), 1)

            def post_qk(i, u):
                t = i * qk.U + u
                dve.wait_ge(sem("q_sq"), t + 1)
                vec.tensor_reduce(QST[:, u % 4, :], QSQ[u % 2][:, :].rearrange("p (h d) -> p h d", h=4), AX.X,
                                  ALU.add).then_inc(sem("q_summed"), 1)
                if not isinstance(t, int) or t >= 1:
                    normalise(*back(qk, i, u, 1))
            run_layer(dve, qk, lo_tile, post_qk, peel=qk.U)
            normalise(*back(qk, qk.T // qk.U, 0, 1))
            run_layer(dve, vl, lo_tile, lambda i, u: None)
            dve.wait_ge(evacuated, vl.n0 + vl.T)
            dve.wait_ge(sem("q_taken"), qk.T)
            vec.memset(STAT[:, 6, :], 0.0).then_inc(sem("hn_dead"), 1)
            vec.memset(STAT[:, 7, :], 0.0).then_inc(sem("ub_free"), TURN)

            def stage_pair(c, y):
                vec.tensor_copy(QS[y][:, :, :], qk_pair(c * 2 + y, 0))
                vec.tensor_copy(KS[y][:, :, :], qk_pair(c * 2 + y, 1)).then_inc(sem("b_staged"), 1)

            def peak(c, u):
                x, b = u // 2, u % 2
                n = (b + 1) * P
                e = ES[b][:, 0:N_GROUPS * n]
                dve.wait_ge(sem("b_scores"), c * NU + (u + 1))
                if b == 0:
                    dve.wait_ge(sem(f"ub_loaded{x}"), c * 48 + 48)
                ins = TTN(e.rearrange("p (g n) -> p g n", g=N_GROUPS),
                          PS[:, b * 1024:b * 1024 + N_GROUPS * n].rearrange("p (g n) -> p g n", g=N_GROUPS),
                          UB[x][:, :, S - n:S], ALU.add)
                ins.then_inc(sem("b_biased"), 1)
                dve.wait_ge(sem("b_biased"), c * NU + (u + 1))
                vec.tensor_reduce(STAT[:, 0, b:b + 1], e, AX.X, ALU.max, negate=True).then_inc(sem("b_max"), 1)
                if b:
                    dve.wait_ge(sem("ub_free"), c * TURN + (TURN + x))
                    vec.memset(STAT[:, 7, :], 0.0).then_inc(sem("ub_free"), 1)

            def take_weights(c, u):
                b = u % 2
                dve.wait_ge(sem("b_T"), c * NU + (u + 1))
                n = 512 if b else N_GROUPS * P
                vec.tensor_copy(ETX[b][:, 0:n], bank[4][:, 0:n]).then_inc(sem("b_ET"), 1)
                vec.reciprocal(STAT[:, 4, b:b + 1], STAT[:, 1, b:b + 1]).then_inc(sem("b_recip"), 1)

            def out(c, u):
                x, b = u // 2, u % 2
                dve.wait_ge(sem("b_recip"), c * NU + (u + 1))
                dve.wait_ge(sem("b_pv"), c * NU + (u + 1))
                TS(OTB[b][:, ds(c * (TURN * HD) + x * HD, HD)], bank[6 + b][:, 0:HD], STAT[:, 4, b:b + 1], None,
                   ALU.mult).then_inc(sem("b_out"), 1)

            def turn(c, last):
                for u in range(NU):
                    if not (last and u >= NU - 2):
                        peak(c + (u + 2) // NU, (u + 2) % NU)
                    elif u < NU - 1:
                        dve.wait_ge(sem("b_out"), c * NU + u)
                    if not (last and u == NU - 1):
                        take_weights(c + (u + 1) // NU, (u + 1) % NU)
                    out(c, u)
                    if u % 4 == 3 and not last:
                        stage_pair(c + 1, u // 4)
            stage_pair(0, 0)
            stage_pair(0, 1)
            peak(0, 0)
            peak(0, 1)
            take_weights(0, 0)
            with dve.Fori(0, HEADS // TURN - 1) as c:
                turn(c, False)
            turn(HEADS // TURN - 1, True)
            dve.wait_ge(sem("ox_hi"), 1)
            TTN(OXL[:, :, :], OX[:, :, :], OXH[:, :, :].bitcast(f32), ALU.subtract).then_inc(sem("ox_lo"), 1)

            update.dve(dve)

        def qk_pair(c, s):
            v = QK[:, :, :, :].rearrange("p (g s) c n -> p s g c n", s=2)[:, s]
            return v[:, :, ds(c, 1), :].rearrange("p g a n -> p g (a n)")
        phase(pool=pool, act=act, pe=pe, dve=dve)

    steps = []
    for row, tag in enumerate("CD"):
        if tag in phases:
            steps += [(ffn, (f"1_{row}",), "norm_ffn1_2", row), ((conv_mixer, attention_mixer)[row], (), "norm_mix_2", row),
                      (ffn, (f"2_{row}",), "norm_ffn2_2", row)]
    norms = [Norm(XN, lambda c, gain=gain, row=row: col(gain, row * DC + c), early=j > 0)
             for j, (_, _, gain, row) in enumerate(steps)]
    for j, (step, args, _, _) in enumerate(steps):
        step(*args, norms[j], norms[j + 1] if j + 1 < len(steps) else None)

    def store(sp):
        if steps:
            for h in range(4):
                sp.wait_ge(sem("added_x"), updates["chunks"] - DC + 2 * h + 2)
                sp.dma_start(out[:, 2 * h:2 * h + 2, :], XT[:, 2 * h:2 * h + 2, :]).then_inc(sem("stored"), 16)
            sp.wait_ge(sem("stored"), 64)
        else:
            sp.wait_ge(sem("x_ready"), updates["whole"])
            sp.dma_start(out, XT[:, :, :]).then_inc(sem("stored"), 16)
            sp.wait_ge(sem("stored"), 16)
    phase(sp=store)

    with nc.Block() as block:
        @block.sync
        def _(sp):
            for part in programs["sp"]:
                part(sp)

        @block.gpsimd
        def _(pool):
            for part in programs["pool"]:
                part(pool)

        @block.scalar
        def _(act):
            own["act"] = Steps(act, sem("act_own"))
            for part in programs["act"]:
                part(act)

        @block.vector
        def _(dve):
            own["dve"] = Steps(dve, sem("dve_own"))
            for part in programs["dve"]:
                part(dve)

        @block.tensor
        def _(pe):
            for part in programs["pe"]:
                part(pe)


def columns(a):
    return np.asarray(a, np.float32).reshape(-1, P).T


def lay_out(inputs):
    a = {k: np.asarray(v) for k, v in inputs.items()}
    small, alibi, onehot = constants()
    packed = []
    for name, n in PARAMS:
        v = a[name]
        if name in ("attn_q_gain_2", "attn_k_gain_2"):
            v = np.tile(v[0], (1, 2))
        packed.append(columns(v))
        assert packed[-1].shape[1] == n, name

    def block_diagonal(w):
        o = np.zeros((2, HD, DC, 2, HD), np.float32)
        for h in range(16):
            o[h % 2, :, h // 2, h % 2, :] = w[h]
        return o.reshape(P, DC, P)

    o = {
        "params": np.concatenate(packed, axis=1),
        "small": small,
        "xT": a["x"][0].T.reshape(DC, P, S).transpose(1, 0, 2),
        "sinks": np.tile(a["attn_sinks"][0], (P, 1)),
        "bd_a": block_diagonal(a["rg_w_a"][0]),
        "bd_x": block_diagonal(a["rg_w_x"][0]),
        "alibi": alibi.reshape(P, HEADS, 2 * P),
        "router_w": a["router_w"][0].reshape(DC, P, NE).transpose(1, 0, 2),
        "router_b": np.tile(a["router_b"][0], (P, 1)),
        "expert_no": np.tile(np.arange(NE, dtype=np.float32), (P, 1)),
        "onehot": onehot,
        "rel_bias_x": np.concatenate([a["rel_bias_2"], np.full((1, N_GROUPS * HEADS), NEG, np.float32)]),
    }
    for k in ("w_ada", "w_in", "w_o_rnn", "w_o_attn", "w_out", "moe_w1", "moe_b1", "moe_w2", "moe_b2",
              "ffn1_w_in_2", "ffn1_w_out_2", "conv_w_in_2", "conv_w_out_2", "attn_w_qkv_2", "attn_w_out_2",
              "ffn2_w_in_2", "ffn2_w_out_2"):
        o[k] = a[k]
    return {k: np.ascontiguousarray(v) for k, v in o.items()}


def kernel(**inputs):
    import concourse.bacc as bacc
    from concourse.bass_utils import run_bass_kernel_spmd

    nc = bacc.Bacc("TRN2", target_bir_lowering=False, num_devices=1)
    arrays, aps = {}, {}
    for name, a in lay_out(inputs).items():
        arrays[f"in_{name}"] = a
        aps[name] = nc.dram_tensor(f"in_{name}", a.shape, mybir.dt.from_np(a.dtype), kind="ExternalInput").ap()
    out = nc.dram_tensor("out_xT", [P, DC, S], mybir.dt.float32, kind="ExternalOutput").ap()
    block_program(nc, aps, out)
    r = run_bass_kernel_spmd(nc, [arrays], core_ids=[0])
    y = np.asarray(r.results[0]["out_xT"])
    return y.transpose(1, 0, 2).reshape(D, S).T.reshape(1, S, D)
```
